# Optimizing a Trainium2 kernel written in Bass

```python
import jax, jax.numpy as jnp
from jax import lax
import numpy as np

D_MODEL = 1024
BATCH = 1
SEQ = 256
DEPTH = 1

RET_HEADS = 4
RET_QK_DIM = 128
RET_V_DIM = 256
RET_CHUNK = 128
MOBA_HEADS = 8
MOBA_HEAD_DIM = 64
MOBA_BLOCK = 256
MOBA_TOPK = 3
MOBA_Q_CHUNK = 16
D_FF = 4 * D_MODEL
NORM_EPS = 1e-6
MASK_VALUE = -1e30

RET_QK_W = RET_HEADS * RET_QK_DIM
RET_V_W = RET_HEADS * RET_V_DIM
MOBA_W = MOBA_HEADS * MOBA_HEAD_DIM
IN_SIZES = [RET_QK_W, RET_QK_W, RET_V_W, RET_V_W, MOBA_W, MOBA_W, MOBA_W, D_MODEL, D_MODEL]
IN_WIDTH = int(sum(IN_SIZES))
SPLIT_IDX = [int(v) for v in np.cumsum(IN_SIZES)[:-1]]

kernel_name = "hybrid_retention_moba_gated_block"

def rms_norm(x, g):
    xf = x.astype(jnp.float32)
    y = xf * lax.rsqrt(jnp.mean(xf * xf, axis=-1, keepdims=True) + NORM_EPS)
    return (y * g.astype(jnp.float32)).astype(x.dtype)

def group_rms(x):
    xf = x.astype(jnp.float32)
    return (xf * lax.rsqrt(jnp.mean(xf * xf, axis=-1, keepdims=True) + NORM_EPS)).astype(x.dtype)

def to_heads(z, n_heads):
    b, t, w = z.shape
    return z.reshape(b, t, n_heads, w // n_heads).transpose(0, 2, 1, 3)

def from_heads(z):
    b, h, t, d = z.shape
    return z.transpose(0, 2, 1, 3).reshape(b, t, h * d)

def retention(q, k, v):
    B, H, T, dk = q.shape
    dv = v.shape[-1]
    C = RET_CHUNK
    N = T // C
    dt = q.dtype
    log_g = jnp.log1p(-jnp.exp2(-5.0 - jnp.arange(H, dtype=jnp.float32)))
    pos = jnp.arange(C, dtype=jnp.float32)
    diff = pos[:, None] - pos[None, :]
    inner_decay = jnp.where(diff >= 0, jnp.exp(log_g[:, None, None] * jnp.maximum(diff, 0.0)), 0.0).astype(dt)
    k_decay = jnp.exp(log_g[:, None] * (C - 1.0 - pos)).astype(dt)
    q_decay = jnp.exp(log_g[:, None] * (pos + 1.0)).astype(dt)
    chunk_decay = jnp.exp(log_g * C).astype(dt)[:, None, None]

    qc = q.reshape(B, H, N, C, dk)
    kc = k.reshape(B, H, N, C, dk) * (dk ** -0.5)
    vc = v.reshape(B, H, N, C, dv)
    scores = jnp.einsum('bhnid,bhnjd->bhnij', qc, kc) * inner_decay[None, :, None]
    inner = jnp.einsum('bhnij,bhnje->bhnie', scores, vc)
    chunk_kv = jnp.einsum('bhnjd,bhnje->nbhde', kc * k_decay[None, :, None, :, None], vc)

    def step(S, kv):
        return S * chunk_decay + kv, S

    _, S_prev = lax.scan(step, jnp.zeros_like(chunk_kv[0]), chunk_kv)
    cross = jnp.einsum('bhnid,nbhde->bhnie', qc * q_decay[None, :, None, :, None], S_prev)
    return (inner + cross).reshape(B, H, T, dv)

def moba_attention(q, k, v):
    B, H, T, d = q.shape
    L = MOBA_BLOCK
    nb = -(-T // L)
    Tp = nb * L
    padw = ((0, 0), (0, 0), (0, Tp - T), (0, 0))
    q = jnp.pad(q, padw)
    k = jnp.pad(k, padw)
    v = jnp.pad(v, padw)
    kb = k.reshape(B, H, nb, L, d)
    vb = v.reshape(B, H, nb, L, d)
    scale = d ** -0.5

    k_mean = jnp.mean(kb.astype(jnp.float32), axis=3)
    gate = jnp.einsum('bhtd,bhnd->bhtn', q.astype(jnp.float32), k_mean)
    q_blk = jnp.arange(Tp) // L
    past = jnp.arange(nb)[None, :] < q_blk[:, None]
    gate = jnp.where(past, gate, -jnp.inf)
    topk = min(MOBA_TOPK, nb)
    g_val, g_idx = lax.top_k(gate, topk)
    sel_valid = jnp.isfinite(g_val)

    slopes = jnp.exp2(-8.0 / H * jnp.arange(1, H + 1, dtype=jnp.float32))
    bi = jnp.arange(B)[:, None, None, None]
    hi = jnp.arange(H)[None, :, None, None]
    offs = jnp.arange(L)
    QC = MOBA_Q_CHUNK

    def chunk(c):
        start = c * QC
        qc = lax.dynamic_slice_in_dim(q, start, QC, axis=2)
        idx = lax.dynamic_slice_in_dim(g_idx, start, QC, axis=2)
        ok = lax.dynamic_slice_in_dim(sel_valid, start, QC, axis=2)
        t_idx = start + jnp.arange(QC)
        ob = start // L
        k_own = lax.dynamic_index_in_dim(kb, ob, axis=2, keepdims=False)
        v_own = lax.dynamic_index_in_dim(vb, ob, axis=2, keepdims=False)
        k_sel = kb[bi, hi, idx]
        v_sel = vb[bi, hi, idx]
        s_own = ob * L + offs
        s_sel = idx[..., None] * L + offs
        d_own = (t_idx[:, None] - s_own[None, :]).astype(jnp.float32)
        d_sel = (t_idx[:, None, None] - s_sel).astype(jnp.float32)
        l_own = jnp.einsum('bhqd,bhsd->bhqs', qc, k_own).astype(jnp.float32) * scale - slopes[:, None, None] * d_own
        l_own = jnp.where(s_own[None, :] <= t_idx[:, None], l_own, MASK_VALUE)
        l_sel = jnp.einsum('bhqd,bhqnsd->bhqns', qc, k_sel).astype(jnp.float32) * scale - slopes[:, None, None, None] * d_sel
        l_sel = jnp.where(ok[..., None], l_sel, MASK_VALUE)
        logits = jnp.concatenate([l_own, l_sel.reshape(B, H, QC, topk * L)], axis=-1)
        p = jax.nn.softmax(logits, axis=-1).astype(v.dtype)
        p_sel = p[..., L:].reshape(B, H, QC, topk, L)
        return (jnp.einsum('bhqs,bhsd->bhqd', p[..., :L], v_own)
                + jnp.einsum('bhqns,bhqnsd->bhqd', p_sel, v_sel))

    out = lax.map(chunk, jnp.arange(Tp // QC))
    out = jnp.moveaxis(out, 0, 2).reshape(B, H, Tp, d)
    return out[:, :, :T]

def setup_inputs(seed: int = 0) -> dict:
    key = jax.random.key(seed)
    ks = jax.random.split(key, 12)
    f32 = jnp.float32

    def w(k, shape, fan_in):
        return jax.random.normal(k, shape, f32) * (fan_in ** -0.5)

    return {
        "x": jax.random.normal(ks[0], (BATCH, SEQ, D_MODEL), f32),
        "norm1_g": 1.0 + 0.02 * jax.random.normal(ks[1], (DEPTH, D_MODEL), f32),
        "w_in": w(ks[2], (DEPTH, D_MODEL, IN_WIDTH), D_MODEL),
        "b_gate": 0.1 * jax.random.normal(ks[3], (DEPTH, 2 * D_MODEL), f32),
        "w_ret_o": w(ks[4], (DEPTH, RET_V_W, D_MODEL), RET_V_W),
        "w_moba_o": w(ks[5], (DEPTH, MOBA_W, D_MODEL), MOBA_W),
        "w_out": w(ks[6], (DEPTH, D_MODEL, D_MODEL), D_MODEL),
        "norm2_g": 1.0 + 0.02 * jax.random.normal(ks[7], (DEPTH, D_MODEL), f32),
        "w_up": w(ks[8], (DEPTH, D_MODEL, D_FF), D_MODEL),
        "w_down": w(ks[9], (DEPTH, D_FF, D_MODEL), D_FF),
        "normf_g": 1.0 + 0.02 * jax.random.normal(ks[10], (D_MODEL,), f32),
    }

def reference(x, norm1_g, w_in, b_gate, w_ret_o, w_moba_o, w_out, norm2_g, w_up, w_down, normf_g):
    for layer in range(DEPTH):
        h = rms_norm(x, norm1_g[layer])
        z = h @ w_in[layer]
        rq, rk, rv, rg, mq, mk, mv, gr, gm = jnp.split(z, SPLIT_IDX, axis=-1)
        ret = retention(to_heads(rq, RET_HEADS), to_heads(rk, RET_HEADS), to_heads(rv, RET_HEADS))
        ret = from_heads(group_rms(ret)) * jax.nn.silu(rg)
        y_ret = ret @ w_ret_o[layer]
        mo = moba_attention(to_heads(mq, MOBA_HEADS), to_heads(mk, MOBA_HEADS), to_heads(mv, MOBA_HEADS))
        y_moba = from_heads(mo) @ w_moba_o[layer]
        bg_r, bg_m = jnp.split(b_gate[layer], 2)
        merged = jax.nn.sigmoid(gr + bg_r) * y_ret + jax.nn.sigmoid(gm + bg_m) * y_moba
        x = x + merged @ w_out[layer]
        h2 = rms_norm(x, norm2_g[layer])
        x = x + jnp.square(jax.nn.relu(h2 @ w_up[layer])) @ w_down[layer]
    return rms_norm(x, normf_g)


_drawn_inputs = setup_inputs


def setup_inputs(seed=0):
    import zlib

    import numpy as np

    out = dict(_drawn_inputs(seed))
    spreads = {}
    factors = {'norm1_g': 3.501, 'b_gate': 3.935, 'norm2_g': 3.295, 'normf_g': 2.907}
    for name, (base, spread) in spreads.items():
        noise = np.random.default_rng([zlib.crc32(name.encode()), seed]).standard_normal(out[name].shape)
        drawn = base * np.exp(spread * noise) if base else spread * noise
        out[name] = __import__('jax').numpy.asarray(drawn.astype(out[name].dtype))
    for name, factor in factors.items():
        out[name] = (out[name] * factor).astype(out[name].dtype)
    return out
```

```python
from contextlib import ExitStack

import concourse.bass as bass
from concourse import mybir

ALU = mybir.AluOpType
ACT = mybir.ActivationFunctionType
AX_X = mybir.AxisListType.X
F32 = mybir.dt.float32
F32R = mybir.dt.float32r

P = 128
T = 256
D = 1024
KD = D // P
RET_HEADS, RET_V = 4, 256
MOBA_HEADS, MOBA_DIM = 8, 64
EPS = 1e-6
RET_SCALE_COLS = RET_HEADS * T
N_CONST = P + RET_SCALE_COLS + 3 * P

SLOTS = 4
AHEAD = SLOTS - 1
UNIT = 2048

U_QK, U_NAT, U_GATE, U_RET, U_MOBA, U_OUT, U_MLP, U_END = 0, 8, 18, 26, 30, 32, 36, 68
O_QK, O_NAT, O_GATE, O_RET, O_MOBA, O_OUT, O_UP = 0, 8, 13, 21, 25, 29, 31
S_QK, S_GATE, S_RET, S_MOBA, S_UP = 0, 8, 16, 20, 24
MLP_CHUNKS = 8
DOWN_A, UP_A, DOWN_B, UP_B = (2, 9), (3, 9), (0, 10), (1, 10)


def constants():
    import numpy as np

    out = np.zeros((P, N_CONST), np.float32)
    out[:, :P] = np.eye(P)
    key = np.arange(P)[:, None]
    query = np.arange(T)[None, :]
    for h in range(RET_HEADS):
        log_g = np.log1p(-np.exp2(-5.0 - h))
        diff = query - key
        decay = np.where(diff >= 0, np.exp(log_g * np.maximum(diff, 0)), 0.0) * P ** -0.5
        out[:, P + h * T:P + (h + 1) * T] = decay
    q, k = np.arange(P)[:, None], np.arange(T)[None, :]
    far = np.float32(1e32)
    out[:, -3 * P:-2 * P] = np.where(k[:, :P] <= q, q - k[:, :P], far)
    out[:, -2 * P:] = np.where(k <= q + P, q + P - k, far)
    return out


def hybrid_block(nc, x, norm1_g, w_in, b_gate, w_ret_o, w_moba_o, w_out, norm2_g, w_up, w_down,
                 normf_g, consts, out):
    x_v = x[0].rearrange("(t p) d -> p t d", p=P)
    out_v = out[0].rearrange("(t p) d -> p t d", p=P)
    w_in_v = w_in[0].rearrange("(k p) n -> p k n", p=P)
    w_ret_v = w_ret_o[0].rearrange("(k p) n -> p k n", p=P)
    w_moba_v = w_moba_o[0].rearrange("(k p) n -> p k n", p=P)
    w_out_v = w_out[0].rearrange("(k p) n -> p k n", p=P)
    w_up_v = w_up[0].rearrange("(k p) n -> p k n", p=P)
    w_down_v = w_down[0].rearrange("(k p) n -> p k n", p=P)

    with ExitStack() as ctx:
        def sb(name, shape, dt=F32):
            return ctx.enter_context(nc.sbuf_tensor(name, shape, dt))

        def sem(name):
            return ctx.enter_context(nc.semaphore(name))

        w_raw = sb("w_raw", [P, SLOTS, UNIT])
        w_hi = sb("w_hi", [P, SLOTS, UNIT], F32R)
        w_lo = sb("w_lo", [P, SLOTS, UNIT], F32R)
        act_a = sb("act_a", [P, KD, 2, T], F32R)
        act_b = sb("act_b", [P, KD, 2, T], F32R)
        act_c = sb("act_c", [P, 4, 2, T], F32R)
        qk = sb("qk", [P, 16, T])
        gates = sb("gates", [P, 16, T])
        nat_a = sb("nat_a", [P, 2, D])
        nat_b = sb("nat_b", [P, 2, D])
        nat_c = sb("nat_c", [P, 2, 512])
        side = sb("side", [P, 2, T])
        scratch = sb("scratch", [P, 3 * P])
        probs_t = sb("probs_t", [P, 3 * P])
        ret_scores = sb("ret_scores", [P, 3 * P])
        ret_junk = sb("ret_junk", [P, RET_V])
        decay = sb("decay", [P, RET_HEADS, T])
        distance = sb("distance", [P, 3 * P])
        ident = sb("ident", [P, P])
        rows = sb("rows", [32, P])
        cols = sb("cols", [P, 32])
        sq = sb("sq", [P, 8])
        ms = sb("ms", [P, 8])
        rstd = sb("rstd", [P, 8])
        neg_half = sb("neg_half", [P, 2])
        top = sb("top", [P, 4])
        neg_top = sb("neg_top", [P, 2])
        prob_sum = sb("prob_sum", [P, 2])
        prob_inv = sb("prob_inv", [P, 2])

        up_sum = qk[:, 0:2, :]
        up_sqr = qk[:, 2:4, :]
        merged = qk[:, 6:8, :]
        branch = qk[:, 4:6, :]
        junk = qk[:, 8:12, :].rearrange("p a b -> p (a b)")
        gf = nat_c[:, :, :].rearrange("p a b -> p (a b)")

        pair = [ctx.enter_context(nc.psum_tensor(f"pair{i}", [P, 2, 512], F32)) for i in range(2)]
        bank = [ctx.enter_context(nc.psum_tensor(f"bank{i}", [P, 512], F32)) for i in range(4, 8)]
        p_logits, p_moba, p_ret, p_retv = bank

        x_loaded = sem("x_loaded")
        small_loaded = sem("small_loaded")
        consts_loaded = sem("consts_loaded")
        x_again = sem("x_again")
        gf_loaded = sem("gf_loaded")
        w_loaded = [sem(f"w_loaded{i}") for i in range(SLOTS)]
        hi_made = sem("hi_made")
        lo_made = sem("lo_made")
        units_used = sem("units_used")
        half_made = sem("half_made")
        out_read = sem("out_read")
        side_made = sem("side_made")
        const_half = sem("const_half")
        sq_made = sem("sq_made")
        ms_made = sem("ms_made")
        rstd_made = sem("rstd_made")
        h_made = sem("h_made")
        cols_t = sem("cols_t")
        cols_made = sem("cols_made")
        xt_made = sem("xt_made")
        xt_hi = sem("xt_hi")
        xt_lo = sem("xt_lo")
        rg_sig = sem("rg_sig")
        dve_step = sem("dve_step")
        act_step = sem("act_step")
        logits_made = sem("logits_made")
        logits_read = sem("logits_read")
        top_made = sem("top_made")
        probs_made = sem("probs_made")
        pt_made = sem("pt_made")
        pt_read = sem("pt_read")
        moba_made = sem("moba_made")
        moba_read = sem("moba_read")
        mt_made = sem("mt_made")
        mt_hi = sem("mt_hi")
        mt_lo = sem("mt_lo")
        rs_made = sem("rs_made")
        rs_read = sem("rs_read")
        rv_made = sem("rv_made")
        ret_sq = sem("ret_sq")
        ret_ms = sem("ret_ms")
        ret_rstd = sem("ret_rstd")
        ret_done = sem("ret_done")
        rt_made = sem("rt_made")
        rt_hi = sem("rt_hi")
        rt_lo = sem("rt_lo")
        gate_sig = sem("gate_sig")
        merged_made = sem("merged_made")
        merged_hi = sem("merged_hi")
        merged_lo = sem("merged_lo")
        x2_made = sem("x2_made")
        x2_sq = sem("x2_sq")
        hid_made = sem("hid_made")
        hid_hi = sem("hid_hi")
        hid_lo = sem("hid_lo")
        down_made = sem("down_made")
        x3_made = sem("x3_made")
        x3_sq = sem("x3_sq")
        x3_ms = sem("x3_ms")
        x3_rstd = sem("x3_rstd")
        y_made = sem("y_made")
        y_stored = sem("y_stored")

        def unit_source(u):
            if u < U_NAT:
                c = 256 * u + (2048 if u >= 4 else 0)
                return w_in_v[:, :, c:c + 256]
            if u < U_GATE:
                n, half = divmod(u - U_NAT, 2)
                c = [2048, 2560, 1024, 1536, 4096][n]
                return w_in_v[:, 4 * half:4 * half + 4, c:c + 512]
            if u < U_RET:
                c = 4608 + 256 * (u - U_GATE)
                return w_in_v[:, :, c:c + 256]
            if u < U_MOBA:
                c = 256 * (u - U_RET)
                return w_ret_v[:, :, c:c + 256]
            if u < U_OUT:
                c = 512 * (u - U_MOBA)
                return w_moba_v[:, :, c:c + 512]
            n, half = divmod(u - U_OUT, 2)
            return w_out_v[:, 4 * half:4 * half + 4, 512 * n:512 * n + 512]

        def unit(u):
            return u % SLOTS, u // SLOTS

        def output_wait(eng, o):
            if o < O_NAT:
                eng.wait_ge(units_used, o + 1)
            elif o < O_GATE:
                eng.wait_ge(units_used, U_NAT + 2 * (o - O_NAT) + 2)
            elif o < O_MOBA:
                eng.wait_ge(units_used, U_GATE + o - O_GATE + 1)
            elif o < O_OUT and (o - O_MOBA) % 2 == 0:
                eng.wait_ge(half_made, (o - O_MOBA) // 2 + 1)
            elif o < O_OUT:
                eng.wait_ge(units_used, U_MOBA + (o - O_MOBA) // 2 + 1)
            else:
                eng.wait_ge(units_used, U_OUT + 2 * (o - O_OUT) + 2)

        def moba_nat(p):
            return qk[:, 8 + p, :].rearrange("p (t n) -> p t n", t=2)

        def wide(ring, slot):
            return ring[:, slot, :].rearrange("p (k n) -> p k n", k=8)

        def mid(ring, slot):
            return ring[:, slot, :].rearrange("p (k n) -> p k n", k=4)

        def long(ring, slot):
            return ring[:, slot, :].rearrange("p (k n) -> p k n", k=2)

        block = ctx.enter_context(nc.Block())

        @block.sync
        def _(sp):
            def load(slot, rnd, view, source):
                if type(rnd) is not int or rnd > 0:
                    sp.wait_ge(lo_made, SLOTS * (rnd - 1) + slot + 1)
                sp.dma_start(view(w_raw, slot), source).then_inc(w_loaded[slot], 16)

            def load_before_mlp(u):
                view = mid if U_NAT <= u < U_GATE or u >= U_MOBA else wide
                load(u % SLOTS, u // SLOTS, view, unit_source(u))

            def load_up(kind, c, half):
                load(kind[0], kind[1] + c, wide, w_up_v[:, :, bass.ds(512 * (c + 1) + 256 * half, 256)])

            def load_down(kind, c, half):
                load(kind[0], kind[1] + c, long, w_down_v[:, bass.ds(4 * c + 2 * half, 2), :])

            for t in range(2):
                sp.dma_start(nat_b[:, t, :], x_v[:, t, :]).then_inc(x_loaded, 16)
            sp.dma_start(ident[:, :], consts[:, 0:P]).then_inc(small_loaded, 16)
            sp.dma_start(rows[0:8, :], norm1_g.rearrange("a (k p) -> (a k) p", p=P)).then_inc(small_loaded, 16)
            sp.dma_start(rows[8:16, :], norm2_g.rearrange("a (k p) -> (a k) p", p=P)).then_inc(small_loaded, 16)
            sp.dma_start(rows[16:32, :], b_gate.rearrange("a (k p) -> (a k) p", p=P)).then_inc(small_loaded, 16)
            for u in range(SLOTS):
                load_before_mlp(u)
            sp.dma_start(decay[:, :, :], consts[:, P:P + RET_SCALE_COLS].rearrange("p (h t) -> p h t", h=RET_HEADS)
                         ).then_inc(consts_loaded, 16)
            sp.dma_start(distance[:, :], consts[:, P + RET_SCALE_COLS:]).then_inc(consts_loaded, 16)
            for u in range(SLOTS, U_OUT):
                load_before_mlp(u)
            sp.wait_ge(rv_made, RET_HEADS)
            sp.dma_start(nat_b[:, :, :], x_v).then_inc(x_again, 16)
            sp.wait_ge(moba_made, MOBA_HEADS)
            sp.dma_start(gf, normf_g.rearrange("(a d) -> a d", a=1).to_broadcast([P, D])).then_inc(gf_loaded, 16)
            for u in range(U_OUT, U_MLP):
                load_before_mlp(u)
            load(0, 9, wide, w_up_v[:, :, 0:256])
            load(1, 9, wide, w_up_v[:, :, 256:512])
            with sp.Fori(0, MLP_CHUNKS - 1) as c:
                load_down(DOWN_A, c, 0)
                load_up(UP_A, c, 0)
                load_down(DOWN_B, c, 1)
                load_up(UP_B, c, 1)
            load(2, 16, long, w_down_v[:, 28:30, :])
            load(3, 16, long, w_down_v[:, 30:32, :])
            for t in range(2):
                sp.wait_ge(y_made, t + 1)
                sp.dma_start(out_v[:, t, :], nat_a[:, t, :]).then_inc(y_stored, 16)
            sp.wait_ge(y_stored, 32)

        @block.gpsimd
        def _(pool):
            nc.gpsimd.memset(neg_half[:, :], -0.5).then_inc(const_half, 1)
            pool.wait_ge(const_half, 1)

            def power(wanted, count, source, made, width):
                pool.wait_ge(wanted, count)
                nc.gpsimd.tensor_tensor(rstd[:, source:source + width], ms[:, source:source + width],
                                        neg_half[:, 0:width], ALU.pow).then_inc(made, 1)

            for t in range(2):
                power(ms_made, t + 1, t, rstd_made, 1)
            for h in range(RET_HEADS):
                if h:
                    pool.wait_ge(ret_done, h)
                power(ret_ms, h + 1, 2, ret_rstd, 2)
            for t in range(2):
                power(x3_ms, t + 1, 6 + t, x3_rstd, 1)

        @block.scalar
        def _(act):
            def make_hi(slot, rnd):
                act.wait_ge(w_loaded[slot], 16 * rnd + 16)
                if type(rnd) is not int or rnd > 0:
                    act.wait_ge(units_used, SLOTS * (rnd - 1) + slot + 1)
                nc.scalar.copy(w_hi[:, slot, :], w_raw[:, slot, :]).then_inc(hi_made, 1)

            def make_side(o):
                output_wait(act, o)
                if o > 0:
                    act.wait_ge(out_read, o)
                nc.scalar.copy(side[:, :, :], pair[o % 2][:, :, T:]).then_inc(side_made, 1)

            for t in range(2):
                act.wait_ge(x_loaded, 16 * (t + 1) if t else 32)
                if t:
                    act.wait_ge(sq_made, 1)
                nc.scalar.activation(junk, nat_b[:, t, :], ACT.Square, accum_out=sq[:, t:t + 1]).then_inc(sq_made, 1)
            make_hi(0, 0)
            act.wait_ge(cols_made, 1)
            for k in range(KD):
                act.wait_ge(xt_made, k // 2 + 1)
                nc.scalar.activation(act_a[:, k, 0, :], bank[k // 2][:, (k % 2) * T:(k % 2) * T + T], ACT.Copy,
                                     scale=cols[:, k:k + 1]).then_inc(xt_hi, 1)
            make_hi(1, 0)
            make_hi(2, 0)

            for u in range(U_QK, U_NAT):
                if u > 0:
                    make_side(O_QK + u - 1)
                make_hi(*unit(u + AHEAD))
            for u in range(U_NAT, U_GATE):
                if u == U_NAT:
                    make_side(O_NAT - 1)
                if u in (U_NAT + 2, U_NAT + 4):
                    n = (u - U_NAT) // 2 - 1
                    output_wait(act, O_NAT + n)
                    nc.scalar.activation(nat_a[:, :, 512 * n:512 * n + 512], pair[(O_NAT + n) % 2][:, :, :],
                                         ACT.Sigmoid).then_inc(rg_sig, 1)
                make_hi(*unit(u + AHEAD))

            def softmax(h):
                act.wait_ge(top_made, h + 1)
                if h:
                    act.wait_ge(moba_read, h)
                for t, (a, b) in enumerate(((0, P), (P, 3 * P))):
                    nc.scalar.activation(scratch[:, a:b], scratch[:, a:b], ACT.Exp, bias=neg_top[:, t:t + 1],
                                         scale=MOBA_DIM ** -0.5, accum_out=prob_sum[:, t:t + 1]
                                         ).then_inc(probs_made, 1)

            def probs_out(h):
                act.wait_ge(pt_made, h + 1)
                if h:
                    act.wait_ge(moba_made, h)
                nc.scalar.copy(probs_t[:, :], p_moba[:, 0:3 * P]).then_inc(pt_read, 1)

            def ret_squares(j):
                act.wait_ge(rv_made, j + 1)
                if j:
                    act.wait_ge(ret_ms, j)
                for t in range(2):
                    if j or t:
                        act.wait_ge(ret_sq, 2 * j + t)
                    nc.scalar.activation(ret_junk[:, :], p_retv[:, t * RET_V:(t + 1) * RET_V], ACT.Square,
                                         accum_out=sq[:, 2 + t:3 + t]).then_inc(ret_sq, 1)

            def ret_hi(j):
                act.wait_ge(rt_made, j + 1)
                nc.scalar.copy(act_b[:, 2 * j:2 * j + 2, 0, :], p_retv[:, :].rearrange("p (k t) -> p k t", k=2)
                               ).then_inc(rt_hi, 1)

            def moba_hi(p):
                act.wait_ge(mt_made, p + 1)
                nc.scalar.copy(act_c[:, p, 0, :], p_ret[:, 0:T]).then_inc(mt_hi, 1)

            for i in range(MOBA_HEADS):
                u = U_GATE + i
                softmax(i)
                if i > 0:
                    make_side(O_GATE + i - 1)
                make_hi(*unit(u + AHEAD))
                probs_out(i)
                if i % 2 == 0:
                    ret_squares(i // 2)
                    if i >= 2:
                        moba_hi(i // 2 - 1)
                else:
                    ret_hi(i // 2)
            for u in range(U_RET, U_MOBA):
                o = u - 1 - U_RET + O_RET
                if u == U_RET:
                    make_side(O_RET - 1)
                    act.wait_ge(out_read, O_RET)
                    for g in range(8):
                        nc.scalar.activation(gates[:, g, :], gates[:, g, :], ACT.Sigmoid,
                                             bias=cols[:, 16 + g:17 + g]).then_inc(gate_sig, 1)
                else:
                    make_side(o)
                make_hi(*unit(u + AHEAD))
                if u == U_RET + 1:
                    moba_hi(3)
                    for g in range(8, 16):
                        nc.scalar.activation(gates[:, g, :], gates[:, g, :], ACT.Sigmoid,
                                             bias=cols[:, 16 + g:17 + g]).then_inc(gate_sig, 1)

            def merged_out(m):
                act.wait_ge(merged_made, m + 1)
                nc.scalar.copy(act_a[:, 2 * m:2 * m + 2, 0, :], merged).then_inc(merged_hi, 1)

            make_side(O_RET + 3)
            make_hi(*unit(U_MOBA + AHEAD))
            make_side(O_MOBA)
            merged_out(0)
            make_side(O_MOBA + 1)
            merged_out(1)
            make_hi(*unit(U_MOBA + 1 + AHEAD))
            make_side(O_MOBA + 2)
            merged_out(2)
            make_side(O_MOBA + 3)
            merged_out(3)

            def x2_squares(n):
                for t in range(2):
                    act.wait_ge(x2_made, 2 * n + t + 1)
                    if n or t:
                        act.wait_ge(x2_sq, 2 * n + t)
                    nc.scalar.activation(junk[:, 0:512], nat_b[:, t, 512 * n:512 * n + 512], ACT.Square,
                                         accum_out=sq[:, 4 + 2 * n + t:5 + 2 * n + t]).then_inc(x2_sq, 1)

            def x2_hi(n):
                for k in range(4 * n, 4 * n + 4):
                    act.wait_ge(xt_made, 4 + k // 2 + 1)
                    nc.scalar.activation(act_b[:, k, 0, :], bank[k // 2][:, (k % 2) * T:(k % 2) * T + T], ACT.Copy,
                                         scale=cols[:, 8 + k:9 + k]).then_inc(xt_hi, 1)

            for u in range(U_OUT, U_OUT + 3):
                make_hi(*unit(u + AHEAD))
            x2_hi(0)
            make_hi(*unit(U_OUT + 3 + AHEAD))
            x2_hi(1)

            def hidden_out(n, half):
                act.wait_ge(hid_made, n + 1)
                nc.scalar.copy(act_c[:, 2 * half:2 * half + 2, 0, :], up_sqr).then_inc(hid_hi, 1)

            def up_side(used, n, half):
                act.wait_ge(units_used, used)
                act.wait_ge(out_read, O_OUT + n)
                nc.scalar.copy(side[:, :, :], pair[(O_UP + half) % 2][:, :, T:]).then_inc(side_made, 1)

            make_hi(*unit(U_MLP + AHEAD))
            x2_squares(0)
            x2_squares(1)
            up_side(U_MLP + 1, 0, 0)
            make_hi(*unit(U_MLP + 1 + AHEAD))
            hidden_out(0, 0)

            def mlp_slots(c, last):
                up_side(38 + 4 * c, 2 * c + 1, 1)
                make_hi(UP_B[0], UP_B[1] + c)
                act.wait_ge(units_used, 37 + 4 * c)
                hidden_out(2 * c + 1, 1)
                make_hi(DOWN_A[0], DOWN_A[1] + 1 + c)
                up_side(40 + 4 * c, 2 * c + 2, 0)
                make_hi(UP_A[0], UP_A[1] + 1 + c)
                act.wait_ge(units_used, 39 + 4 * c)
                hidden_out(2 * c + 2, 0)
                if not last:
                    make_hi(DOWN_B[0], DOWN_B[1] + 1 + c)

            with act.Fori(0, MLP_CHUNKS - 2) as c:
                mlp_slots(c, False)
            mlp_slots(MLP_CHUNKS - 2, True)
            up_side(38 + 4 * (MLP_CHUNKS - 1), 2 * MLP_CHUNKS - 1, 1)
            act.wait_ge(units_used, 37 + 4 * (MLP_CHUNKS - 1))
            hidden_out(2 * MLP_CHUNKS - 1, 1)
            for t in range(2):
                act.wait_ge(x3_made, 2 * t + 2)
                if t:
                    act.wait_ge(x3_sq, 1)
                nc.scalar.activation(junk, nat_a[:, t, :], ACT.Square, accum_out=sq[:, t:t + 1]).then_inc(x3_sq, 1)

        @block.vector
        def _(dve):
            steps = [0]

            def link(ins):
                steps[0] += 1
                ins.then_inc(dve_step, 1)
                dve.wait_ge(dve_step, steps[0])

            def make_lo(slot, rnd):
                dve.wait_ge(hi_made, SLOTS * rnd + slot + 1)
                nc.vector.tensor_tensor(w_lo[:, slot, :], w_raw[:, slot, :], w_hi[:, slot, :].bitcast(F32),
                                        ALU.subtract).then_inc(lo_made, 1)

            def add_side(o, s, parity, into):
                dve.wait_ge(side_made, s + 1)
                nc.vector.tensor_tensor(into, pair[parity][:, :, 0:T], side[:, :, :], ALU.add).then_inc(out_read, 1)

            for t in range(2):
                dve.wait_ge(sq_made, t + 1)
                nc.vector.tensor_scalar(ms[:, t:t + 1], sq[:, t:t + 1], 1.0 / D, EPS, ALU.mult, ALU.add
                                        ).then_inc(ms_made, 1)
                dve.wait_ge(rstd_made, t + 1)
                nc.vector.tensor_scalar(nat_a[:, t, :], nat_b[:, t, :], rstd[:, t:t + 1], None, ALU.mult
                                        ).then_inc(h_made, 1)
            dve.wait_ge(cols_t, 1)
            nc.vector.tensor_copy(cols[:, :], pair[1][:, 0, 0:32]).then_inc(cols_made, 1)
            make_lo(0, 0)
            dve.wait_ge(cols_made, 1)
            for k in range(KD):
                dve.wait_ge(xt_hi, k // 2 * 2 + 2)
                nc.vector.scalar_tensor_tensor(out=act_a[:, k, 1, :], in0=bank[k // 2][:, (k % 2) * T:(k % 2) * T + T],
                                               scalar=cols[:, k:k + 1], in1=act_a[:, k, 0, :].bitcast(F32),
                                               op0=ALU.mult, op1=ALU.subtract).then_inc(xt_lo, 1)
            make_lo(1, 0)
            make_lo(2, 0)

            for u in range(U_QK, U_NAT):
                if u > 0:
                    add_side(O_QK + u - 1, S_QK + u - 1, (u - 1) % 2, qk[:, 2 * u - 2:2 * u, :])
                make_lo(*unit(u + AHEAD))

            def natural_out(n):
                o = O_NAT + n
                source = pair[o % 2][:, :, :]
                if n < 2:
                    part = nat_a[:, :, 512 * n:512 * n + 512]
                    dve.wait_ge(rg_sig, n + 1)
                    nc.vector.tensor_tensor(part, source, part, ALU.mult).then_inc(out_read, 1)
                    return
                output_wait(dve, o)
                if n < 4:
                    nc.vector.tensor_copy(nat_b[:, :, 512 * (n - 2):512 * (n - 2) + 512], source).then_inc(out_read, 1)
                else:
                    nc.vector.tensor_copy(nat_c[:, :, :], source).then_inc(out_read, 1)

            for u in range(U_NAT, U_GATE):
                if u == U_NAT:
                    add_side(O_NAT - 1, S_GATE - 1, 1, qk[:, 14:16, :])
                elif (u - U_NAT) % 2 == 0:
                    natural_out((u - U_NAT) // 2 - 1)
                make_lo(*unit(u + AHEAD))
            natural_out(4)

            def logits(h):
                dve.wait_ge(logits_made, h + 1)
                if h == 0:
                    dve.wait_ge(consts_loaded, 32)
                else:
                    dve.wait_ge(pt_made, h)
                slope = 2.0 ** -(h + 1)
                nc.vector.scalar_tensor_tensor(out=scratch[:, :], in0=distance[:, :], scalar=-slope * MOBA_DIM ** 0.5,
                                               in1=p_logits[:, 0:3 * P], op0=ALU.mult, op1=ALU.add
                                               ).then_inc(logits_read, 1)
                dve.wait_ge(logits_read, h + 1)
                nc.vector.reduce_max(top[:, 0:1], scratch[:, 0:P], AX_X).then_inc(dve_step, 1)
                steps[0] += 1
                link(nc.vector.reduce_max(top[:, 1:2], scratch[:, P:3 * P], AX_X))
                nc.vector.tensor_scalar(neg_top[:, :], top[:, 0:2], -MOBA_DIM ** -0.5, None, ALU.mult
                                        ).then_inc(top_made, 1)

            def decayed(j):
                dve.wait_ge(rs_made, j + 1)
                if j:
                    dve.wait_ge(rv_made, j)
                for a, b in ((0, T), (T, T + P)):
                    nc.vector.tensor_tensor(ret_scores[:, a:b], p_ret[:, a:b], decay[:, j, 0:b - a], ALU.mult
                                            ).then_inc(rs_read, 1)

            def moba_norm(h):
                dve.wait_ge(probs_made, 2 * h + 2)
                link(nc.vector.reciprocal(prob_inv[:, :], prob_sum[:, :]))
                dve.wait_ge(moba_made, h + 1)
                for t in range(2):
                    ins = nc.vector.tensor_scalar(moba_nat(h // 2)[:, t, (h % 2) * MOBA_DIM:(h % 2 + 1) * MOBA_DIM],
                                                  p_moba[:, t * MOBA_DIM:(t + 1) * MOBA_DIM],
                                                  prob_inv[:, t:t + 1], None, ALU.mult)
                    if t == 0:
                        link(ins)
                    else:
                        ins.then_inc(moba_read, 1)

            def ret_norm(j):
                dve.wait_ge(ret_sq, 2 * j + 2)
                nc.vector.tensor_scalar(ms[:, 2:4], sq[:, 2:4], 1.0 / RET_V, EPS, ALU.mult, ALU.add
                                        ).then_inc(ret_ms, 1)
                dve.wait_ge(ret_rstd, j + 1)
                for t in range(2):
                    part = nat_a[:, t, j * RET_V:(j + 1) * RET_V]
                    ins = nc.vector.scalar_tensor_tensor(out=part, in0=p_retv[:, t * RET_V:(t + 1) * RET_V],
                                                         scalar=rstd[:, 2 + t:3 + t], in1=part,
                                                         op0=ALU.mult, op1=ALU.mult)
                    if t == 0:
                        link(ins)
                    else:
                        ins.then_inc(ret_done, 1)

            def ret_lo(j):
                dve.wait_ge(rt_hi, j + 1)
                nc.vector.tensor_tensor(act_b[:, 2 * j:2 * j + 2, 1, :], p_retv[:, :].rearrange("p (k t) -> p k t", k=2),
                                        act_b[:, 2 * j:2 * j + 2, 0, :].bitcast(F32), ALU.subtract).then_inc(rt_lo, 1)

            def moba_lo(p):
                dve.wait_ge(mt_hi, p + 1)
                nc.vector.tensor_tensor(act_c[:, p, 1, :], p_ret[:, 0:T], act_c[:, p, 0, :].bitcast(F32),
                                        ALU.subtract).then_inc(mt_lo, 1)

            for i in range(MOBA_HEADS):
                u = U_GATE + i
                logits(i)
                if i % 2 == 0:
                    decayed(i // 2)
                if i > 0:
                    moba_norm(i - 1)
                    o = O_GATE + i - 1
                    add_side(o, S_GATE + i - 1, o % 2, gates[:, 2 * i - 2:2 * i, :])
                make_lo(*unit(u + AHEAD))
                if i % 2 == 0:
                    ret_norm(i // 2)
                    if i >= 2:
                        moba_lo(i // 2 - 1)
                else:
                    ret_lo(i // 2)

            def gated(o, pair_of_tiles, first_gate):
                n = pair_of_tiles
                add_side(o, S_RET + o - O_RET, o % 2, branch)
                dve.wait_ge(out_read, o + 1)
                g = gates[:, first_gate + 2 * n:first_gate + 2 * n + 2, :]
                dve.wait_ge(gate_sig, first_gate + 2 * n + 2)
                link(nc.vector.tensor_tensor(g, branch, g, ALU.mult))

            for u in range(U_RET, U_MOBA):
                if u == U_RET:
                    moba_norm(MOBA_HEADS - 1)
                    o = O_RET - 1
                    add_side(o, S_RET - 1, o % 2, gates[:, 14:16, :])
                else:
                    gated(u - 1 - U_RET + O_RET, u - 1 - U_RET, 0)
                make_lo(*unit(u + AHEAD))
                if u == U_RET + 1:
                    moba_lo(3)

            def merge(m):
                if m:
                    dve.wait_ge(merged_lo, m)
                gated(O_MOBA + m, m, 8)
                nc.vector.tensor_tensor(merged, gates[:, 2 * m:2 * m + 2, :],
                                        gates[:, 8 + 2 * m:10 + 2 * m, :], ALU.add).then_inc(merged_made, 1)

            def merged_lo_of(m):
                dve.wait_ge(merged_hi, m + 1)
                nc.vector.tensor_tensor(act_a[:, 2 * m:2 * m + 2, 1, :], merged,
                                        act_a[:, 2 * m:2 * m + 2, 0, :].bitcast(F32), ALU.subtract
                                        ).then_inc(merged_lo, 1)

            gated(O_RET + 3, 3, 0)
            make_lo(*unit(U_MOBA + AHEAD))
            merge(0)
            merged_lo_of(0)
            merge(1)
            merged_lo_of(1)
            make_lo(*unit(U_MOBA + 1 + AHEAD))
            merge(2)
            merged_lo_of(2)
            merge(3)
            merged_lo_of(3)

            def residual(n):
                o = O_OUT + n
                output_wait(dve, o)
                for t in range(2):
                    part = nat_b[:, t, 512 * n:512 * n + 512]
                    nc.vector.tensor_tensor(part, pair[o % 2][:, t, :], part, ALU.add).then_inc(x2_made, 1)

            def x2_lo(n):
                for k in range(4 * n, 4 * n + 4):
                    dve.wait_ge(xt_hi, KD + k // 2 * 2 + 2)
                    nc.vector.scalar_tensor_tensor(out=act_b[:, k, 1, :],
                                                   in0=bank[k // 2][:, (k % 2) * T:(k % 2) * T + T],
                                                   scalar=cols[:, 8 + k:9 + k], in1=act_b[:, k, 0, :].bitcast(F32),
                                                   op0=ALU.mult, op1=ALU.subtract).then_inc(xt_lo, 1)

            dve.wait_ge(x_again, 16)
            make_lo(*unit(U_OUT + AHEAD))
            make_lo(*unit(U_OUT + 1 + AHEAD))
            residual(0)
            make_lo(*unit(U_OUT + 2 + AHEAD))
            x2_lo(0)
            make_lo(*unit(U_OUT + 3 + AHEAD))
            residual(1)
            x2_lo(1)

            def hidden_sum(n, half):
                add_side(None, S_UP + n, (O_UP + half) % 2, up_sum)
                dve.wait_ge(out_read, O_OUT + n + 1)
                nc.vector.scalar_tensor_tensor(out=up_sqr, in0=up_sum, scalar=0.0, in1=up_sum,
                                               op0=ALU.max, op1=ALU.mult).then_inc(hid_made, 1)

            def hidden_lo(n, half):
                dve.wait_ge(hid_hi, n + 1)
                nc.vector.tensor_tensor(act_c[:, 2 * half:2 * half + 2, 1, :], up_sqr,
                                        act_c[:, 2 * half:2 * half + 2, 0, :].bitcast(F32), ALU.subtract
                                        ).then_inc(hid_lo, 1)

            make_lo(*unit(U_MLP + AHEAD))
            hidden_sum(0, 0)
            make_lo(*unit(U_MLP + 1 + AHEAD))
            hidden_lo(0, 0)

            def mlp_slots(c, last):
                dve.wait_ge(hid_lo, 2 * c + 1)
                hidden_sum(2 * c + 1, 1)
                make_lo(UP_B[0], UP_B[1] + c)
                hidden_lo(2 * c + 1, 1)
                make_lo(DOWN_A[0], DOWN_A[1] + 1 + c)
                dve.wait_ge(hid_lo, 2 * c + 2)
                hidden_sum(2 * c + 2, 0)
                make_lo(UP_A[0], UP_A[1] + 1 + c)
                hidden_lo(2 * c + 2, 0)
                if not last:
                    make_lo(DOWN_B[0], DOWN_B[1] + 1 + c)

            with dve.Fori(0, MLP_CHUNKS - 2) as c:
                mlp_slots(c, False)
            mlp_slots(MLP_CHUNKS - 2, True)
            dve.wait_ge(hid_lo, 2 * MLP_CHUNKS - 1)
            hidden_sum(2 * MLP_CHUNKS - 1, 1)
            hidden_lo(2 * MLP_CHUNKS - 1, 1)

            dve.wait_ge(x2_sq, 4)
            link(nc.vector.tensor_tensor(ms[:, 4:6], sq[:, 4:6], sq[:, 6:8], ALU.add))
            link(nc.vector.tensor_scalar(ms[:, 4:6], ms[:, 4:6], 1.0 / D, EPS, ALU.mult, ALU.add))
            link(nc.vector.reciprocal(rstd[:, 4:6], ms[:, 4:6]))
            dve.wait_ge(gf_loaded, 16)
            for t in range(2):
                dve.wait_ge(down_made, t + 1)
                for n in range(2):
                    nc.vector.scalar_tensor_tensor(out=nat_a[:, t, 512 * n:512 * n + 512], in0=bank[2 * t + n][:, :],
                                                   scalar=rstd[:, 4 + t:5 + t],
                                                   in1=nat_b[:, t, 512 * n:512 * n + 512],
                                                   op0=ALU.mult, op1=ALU.add).then_inc(x3_made, 1)
            for t in range(2):
                dve.wait_ge(x3_sq, t + 1)
                nc.vector.tensor_scalar(ms[:, 6 + t:7 + t], sq[:, t:t + 1], 1.0 / D, EPS, ALU.mult, ALU.add
                                        ).then_inc(x3_ms, 1)
                dve.wait_ge(x3_rstd, t + 1)
                nc.vector.scalar_tensor_tensor(out=nat_a[:, t, :], in0=nat_a[:, t, :], scalar=rstd[:, 6 + t:7 + t],
                                               in1=gf, op0=ALU.mult, op1=ALU.mult).then_inc(y_made, 1)

        @block.tensor
        def _(pe):
            def transposed(view_hi, view_lo, moving, col, into, ready=None):
                k_tiles = view_hi.shape[1]
                for k in range(k_tiles):
                    if ready:
                        made, before, tiles = ready
                        if k % tiles == 0:
                            pe.wait_ge(made, before + k // tiles + 1)
                    whole = (into[:, :], view_hi[:, k, col:col + P], moving[:, k, :, :])
                    left = (into[:, 0:T], view_lo[:, k, col:col + P], moving[:, k, 0, :])
                    if k < k_tiles - 1:
                        nc.tensor.matmul(*whole, start=(k == 0), stop=False)
                        nc.tensor.matmul(*left, start=False, stop=False)
                    else:
                        nc.tensor.matmul(*left, start=False, stop=False)
                        ins = nc.tensor.matmul(*whole, start=False, stop=True)
                return ins

            def unit_ready(slot, rnd):
                pe.wait_ge(lo_made, SLOTS * rnd + slot + 1)

            def output_free(o):
                if o >= 2:
                    pe.wait_ge(out_read, o - 1)

            def wide_unit(slot, rnd, moving, parity, ready=None):
                unit_ready(slot, rnd)
                hi, lo = wide(w_hi, slot), wide(w_lo, slot)
                transposed(hi, lo, moving, 0, pair[parity][:, 0, :], ready)
                transposed(hi, lo, moving, P, pair[parity][:, 1, :]).then_inc(units_used, 1)

            def natural_unit(u, moving, parity, half):
                slot = u % SLOTS
                unit_ready(*unit(u))
                hi, lo = mid(w_hi, slot), mid(w_lo, slot)
                for t in range(2):
                    for k in range(4):
                        for n, (part, w) in enumerate(((0, hi), (0, lo), (1, hi))):
                            ins = nc.tensor.matmul(pair[parity][:, t, :],
                                                   moving[:, 4 * half + k, part, t * P:(t + 1) * P], w[:, k, :],
                                                   start=(half == 0 and k == 0 and n == 0),
                                                   stop=(half == 1 and k == 3 and n == 2))
                ins.then_inc(units_used, 1)

            pe.wait_ge(small_loaded, 64)
            nc.tensor.transpose(pair[1][:, 0, 0:32], rows[:, :], ident[0:32, 0:32]).then_inc(cols_t, 1)
            for t in range(2):
                pe.wait_ge(h_made, t + 1)
                for k in range(KD):
                    ins = nc.tensor.transpose(bank[k // 2][:, (k % 2) * T + t * P:(k % 2) * T + (t + 1) * P],
                                              nat_a[:, t, k * P:(k + 1) * P], ident[:, :])
                    if t == 1 and k % 2 == 1:
                        ins.then_inc(xt_made, 1)

            for u in range(U_QK, U_NAT):
                o = O_QK + u
                output_free(o)
                if u == 1:
                    pe.wait_ge(cols_made, 1)
                wide_unit(*unit(u), act_a, o % 2, (xt_lo, 0, 1) if u == 0 else None)
            for u in range(U_NAT, U_GATE):
                n, half = divmod(u - U_NAT, 2)
                o = O_NAT + n
                if half == 0:
                    output_free(o)
                natural_unit(u, act_a, o % 2, half)

            def moba_scores(h):
                if h:
                    pe.wait_ge(logits_read, h)
                a, q, k = (h % 2) * MOBA_DIM, 8 + h // 2, 12 + h // 2
                nc.tensor.matmul(p_logits[:, 0:P], qk[a:a + MOBA_DIM, q, 0:P], qk[a:a + MOBA_DIM, k, 0:P],
                                 start=True, stop=True)
                nc.tensor.matmul(p_logits[:, P:3 * P], qk[a:a + MOBA_DIM, q, P:T], qk[a:a + MOBA_DIM, k, :],
                                 start=True, stop=True).then_inc(logits_made, 1)

            def moba_transposes(h):
                pe.wait_ge(probs_made, 2 * h + 2)
                if h:
                    pe.wait_ge(moba_read, h)
                for b in range(3):
                    ins = nc.tensor.transpose(p_moba[:, b * P:(b + 1) * P], scratch[:, b * P:(b + 1) * P], ident[:, :])
                ins.then_inc(pt_made, 1)

            def moba_values(h):
                pe.wait_ge(pt_read, h + 1)
                v = nat_c[:, :, h * MOBA_DIM:(h + 1) * MOBA_DIM]
                nc.tensor.matmul(p_moba[:, 0:MOBA_DIM], probs_t[:, 0:P], v[:, 0, :], start=True, stop=True)
                nc.tensor.matmul(p_moba[:, MOBA_DIM:P], probs_t[:, P:2 * P], v[:, 0, :], start=True, stop=False)
                nc.tensor.matmul(p_moba[:, MOBA_DIM:P], probs_t[:, 2 * P:3 * P], v[:, 1, :], start=False, stop=True
                                 ).then_inc(moba_made, 1)

            def moba_turn(p):
                pe.wait_ge(moba_read, 2 * p + 2)
                pe.wait_ge(rs_read, min(2 * p + 4, 2 * RET_HEADS))
                for t in range(2):
                    ins = nc.tensor.transpose(p_ret[:, t * P:(t + 1) * P], moba_nat(p)[:, t, :], ident[:, :])
                ins.then_inc(mt_made, 1)

            def ret_scores_of(j):
                if j >= 2:
                    pe.wait_ge(mt_lo, j - 1)
                if j >= 1:
                    pe.wait_ge(rs_read, 2 * j)
                nc.tensor.matmul(p_ret[:, 0:T], qk[:, 4 + j, 0:P], qk[:, j, :], start=True, stop=True)
                nc.tensor.matmul(p_ret[:, T:T + P], qk[:, 4 + j, P:T], qk[:, j, P:T], start=True, stop=True
                                 ).then_inc(rs_made, 1)

            def ret_values(j):
                pe.wait_ge(rs_read, 2 * j + 2)
                if j:
                    pe.wait_ge(rt_lo, j)
                v = nat_b[:, :, j * RET_V:(j + 1) * RET_V]
                nc.tensor.matmul(p_retv[:, 0:RET_V], ret_scores[:, 0:P], v[:, 0, :], start=True, stop=True)
                nc.tensor.matmul(p_retv[:, RET_V:], ret_scores[:, P:T], v[:, 0, :], start=True, stop=False)
                nc.tensor.matmul(p_retv[:, RET_V:], ret_scores[:, T:T + P], v[:, 1, :], start=False, stop=True
                                 ).then_inc(rv_made, 1)

            def ret_turn(j):
                pe.wait_ge(ret_done, j + 1)
                for k in range(2):
                    for t in range(2):
                        a = j * RET_V + k * P
                        ins = nc.tensor.transpose(p_retv[:, k * T + t * P:k * T + (t + 1) * P],
                                                  nat_a[:, t, a:a + P], ident[:, :])
                ins.then_inc(rt_made, 1)

            pe.wait_ge(out_read, O_QK + 8)
            pe.wait_ge(xt_lo, KD)
            moba_scores(0)
            ret_scores_of(0)
            for i in range(MOBA_HEADS):
                output_free(O_GATE + i)
                wide_unit(*unit(U_GATE + i), act_a, (O_GATE + i) % 2)
                moba_transposes(i)
                if i == 0:
                    pe.wait_ge(out_read, O_GATE)
                if i % 2 == 0:
                    ret_values(i // 2)
                    if i >= 2:
                        moba_turn(i // 2 - 1)
                else:
                    ret_turn(i // 2)
                if i + 1 < MOBA_HEADS:
                    moba_scores(i + 1)
                    if i % 2 == 1:
                        ret_scores_of(i // 2 + 1)
                moba_values(i)

            for u in range(U_RET, U_MOBA):
                o = O_RET + u - U_RET
                output_free(o)
                wide_unit(*unit(u), act_b, o % 2, (rt_lo, 0, 2) if u == U_RET else None)
                if u == U_RET:
                    moba_turn(3)

            for u in range(U_MOBA, U_OUT):
                slot = u % SLOTS
                unit_ready(*unit(u))
                for n in range(4):
                    o = O_MOBA + 2 * (u - U_MOBA) + n // 2
                    if n % 2 == 0:
                        output_free(o)
                    if u == U_MOBA and n == 0:
                        pe.wait_ge(mt_lo, 4)
                    ins = transposed(mid(w_hi, slot), mid(w_lo, slot), act_c, n * P, pair[o % 2][:, n % 2, :])
                    if n == 1:
                        ins.then_inc(half_made, 1)
                ins.then_inc(units_used, 1)

            def x2_turn(n):
                for t in range(2):
                    pe.wait_ge(x2_made, 2 * n + t + 1)
                    for k in range(4 * n, 4 * n + 4):
                        ins = nc.tensor.transpose(bank[k // 2][:, (k % 2) * T + t * P:(k % 2) * T + (t + 1) * P],
                                                  nat_b[:, t, k * P:(k + 1) * P], ident[:, :])
                        if t == 1 and k % 2 == 1:
                            ins.then_inc(xt_made, 1)

            for u in range(U_OUT, U_MLP):
                n, half = divmod(u - U_OUT, 2)
                if half == 0:
                    output_free(O_OUT + n)
                pe.wait_ge(merged_lo, 2 * half + 2)
                natural_unit(u, act_a, (O_OUT + n) % 2, half)
                if u == U_OUT + 2:
                    x2_turn(0)
            x2_turn(1)

            def up_unit(kind, c, n, half, ready=None):
                wide_unit(kind[0], kind[1] + c, act_b, (O_UP + half) % 2, ready)

            def down_unit(kind, c, half, first=False, final=False):
                slot = kind[0]
                unit_ready(slot, kind[1] + c)
                pe.wait_ge(hid_lo, 2 * c + 1 + half)
                hi, lo = long(w_hi, slot), long(w_lo, slot)
                for t in range(2):
                    for f in range(2):
                        def stationary(part):
                            return act_c[:, 2 * half + f, part, t * P:(t + 1) * P]
                        for m, (part, w, n) in enumerate(((0, hi, 0), (0, lo, 0), (0, hi, 1), (0, lo, 1),
                                                          (1, hi, 0), (1, hi, 1))):
                            ins = nc.tensor.matmul(bank[2 * t + n][:, :], stationary(part),
                                                   w[:, f, n * 512:(n + 1) * 512],
                                                   start=(first and f == 0 and m in (0, 2)),
                                                   stop=(final and f == 1 and m in (4, 5)))
                    if final:
                        ins.then_inc(down_made, 1)
                if not final:
                    ins.then_inc(units_used, 1)

            pe.wait_ge(x2_made, 2)
            up_unit(unit(U_MLP), 0, 0, 0, (xt_lo, KD, 1))
            pe.wait_ge(x2_made, 4)
            up_unit(unit(U_MLP + 1), 0, 1, 1)

            def mlp_round(c, first):
                down_unit(DOWN_A, c, 0, first=first)
                pe.wait_ge(out_read, O_OUT + 2 * c + 1)
                up_unit(UP_A, c, 2 * c + 2, 0)
                down_unit(DOWN_B, c, 1)
                pe.wait_ge(out_read, O_OUT + 2 * c + 2)
                up_unit(UP_B, c, 2 * c + 3, 1)

            mlp_round(0, True)
            with pe.Fori(1, MLP_CHUNKS - 1) as c:
                mlp_round(c, False)
            down_unit(DOWN_A, MLP_CHUNKS - 1, 0)
            down_unit((3, 9), MLP_CHUNKS - 1, 1, final=True)


def kernel(x, norm1_g, w_in, b_gate, w_ret_o, w_moba_o, w_out, norm2_g, w_up, w_down, normf_g):
    import numpy as np

    import concourse.bacc as bacc
    from concourse.bass_utils import run_bass_kernel_spmd

    given = {
        "x": x, "norm1_g": norm1_g, "w_in": w_in, "b_gate": b_gate, "w_ret_o": w_ret_o, "w_moba_o": w_moba_o,
        "w_out": w_out, "norm2_g": norm2_g, "w_up": w_up, "w_down": w_down, "normf_g": normf_g,
        "consts": constants(),
    }
    nc = bacc.Bacc("TRN2", target_bir_lowering=False, num_devices=1)
    arrays, args = {}, []
    for name, value in given.items():
        a = np.ascontiguousarray(value)
        arrays[f"{name}_dram"] = a
        args.append(nc.dram_tensor(f"{name}_dram", a.shape, mybir.dt.from_np(a.dtype), kind="ExternalInput").ap())
    args.append(nc.dram_tensor("out_dram", (1, T, D), F32, kind="ExternalOutput").ap())
    hybrid_block(nc, *args)
    r = run_bass_kernel_spmd(nc, [arrays], core_ids=[0])
    return r.results[0]["out_dram"]
```

```python
from contextlib import ExitStack

import concourse.bass as bass
from concourse import mybir

ALU = mybir.AluOpType
ACT = mybir.ActivationFunctionType
AX_X = mybir.AxisListType.X
F32 = mybir.dt.float32
F32R = mybir.dt.float32r

P = 128
T = 256
D = 1024
KD = D // P
RET_HEADS, RET_V = 4, 256
MOBA_HEADS, MOBA_DIM = 8, 64
EPS = 1e-6
RET_SCALE_COLS = RET_HEADS * T
N_CONST = P + RET_SCALE_COLS + 3 * P

SLOTS = 4
AHEAD = SLOTS - 1
UNIT = 2048

U_QK, U_NAT, U_GATE, U_RET, U_MOBA, U_OUT, U_MLP, U_END = 0, 8, 18, 26, 30, 32, 36, 68
O_QK, O_NAT, O_GATE, O_RET, O_MOBA, O_OUT, O_UP = 0, 8, 13, 21, 25, 29, 31
S_QK, S_GATE, S_RET, S_MOBA, S_UP = 0, 8, 16, 20, 24
MLP_CHUNKS = 8
WARM_UP = 8
DOWN_A, UP_A, DOWN_B, UP_B = (2, 9), (3, 9), (0, 10), (1, 10)


def constants():
    import numpy as np

    out = np.zeros((P, N_CONST), np.float32)
    out[:, :P] = np.eye(P)
    key = np.arange(P)[:, None]
    query = np.arange(T)[None, :]
    for h in range(RET_HEADS):
        log_g = np.log1p(-np.exp2(-5.0 - h))
        diff = query - key
        decay = np.where(diff >= 0, np.exp(log_g * np.maximum(diff, 0)), 0.0) * P ** -0.5
        out[:, P + h * T:P + (h + 1) * T] = decay
    q, k = np.arange(P)[:, None], np.arange(T)[None, :]
    far = np.float32(1e32)
    out[:, -3 * P:-2 * P] = np.where(k[:, :P] <= q, q - k[:, :P], far)
    out[:, -2 * P:] = np.where(k <= q + P, q + P - k, far)
    return out


def hybrid_block(nc, x, norm1_g, w_in, b_gate, w_ret_o, w_moba_o, w_out, norm2_g, w_up, w_down,
                 normf_g, consts, out):
    x_v = x[0].rearrange("(t p) d -> p t d", p=P)
    out_v = out[0].rearrange("(t p) d -> p t d", p=P)
    w_in_v = w_in[0].rearrange("(k p) n -> p k n", p=P)
    w_ret_v = w_ret_o[0].rearrange("(k p) n -> p k n", p=P)
    w_moba_v = w_moba_o[0].rearrange("(k p) n -> p k n", p=P)
    w_out_v = w_out[0].rearrange("(k p) n -> p k n", p=P)
    w_up_v = w_up[0].rearrange("(k p) n -> p k n", p=P)
    w_down_v = w_down[0].rearrange("(k p) n -> p k n", p=P)

    with ExitStack() as ctx:
        def sb(name, shape, dt=F32):
            return ctx.enter_context(nc.sbuf_tensor(name, shape, dt))

        def sem(name):
            return ctx.enter_context(nc.semaphore(name))

        w_raw = sb("w_raw", [P, SLOTS, UNIT])
        w_hi = sb("w_hi", [P, SLOTS, UNIT], F32R)
        w_lo = sb("w_lo", [P, SLOTS, UNIT], F32R)
        act_a = sb("act_a", [P, KD, 2, T], F32R)
        act_b = sb("act_b", [P, KD, 2, T], F32R)
        act_c = sb("act_c", [P, 4, 2, T], F32R)
        qk = sb("qk", [P, 16, T])
        gates = sb("gates", [P, 16, T])
        nat_a = sb("nat_a", [P, 2, D])
        nat_b = sb("nat_b", [P, 2, D])
        nat_c = sb("nat_c", [P, 2, 512])
        side = sb("side", [P, 2, T])
        scratch = sb("scratch", [P, 3 * P])
        probs_t = sb("probs_t", [P, 3 * P])
        ret_scores = sb("ret_scores", [P, 3 * P])
        ret_junk = sb("ret_junk", [P, RET_V])
        decay = sb("decay", [P, RET_HEADS, T])
        distance = sb("distance", [P, 3 * P])
        moba_out = sb("moba_out", [P, T])
        zeros = sb("zeros", [P, T])
        ident = sb("ident", [P, P])
        g1_rows = sb("g1_rows", [8, P])
        rows = sb("rows", [24, P])
        cols = sb("cols", [P, 32])
        sq = sb("sq", [P, 8])
        ms = sb("ms", [P, 8])
        rstd = sb("rstd", [P, 8])
        neg_half = sb("neg_half", [P, 2])
        top = sb("top", [P, 4])
        neg_top = sb("neg_top", [P, 2])
        prob_sum = sb("prob_sum", [P, 2])
        prob_inv = sb("prob_inv", [P, 2])

        up_sum = qk[:, 0:2, :]
        up_sqr = qk[:, 2:4, :]
        merged = qk[:, 8:12, :].rearrange("p (m k) t -> p m k t", m=2)
        branch = qk[:, 4:6, :]
        junk = qk[:, 8:12, :].rearrange("p a b -> p (a b)")
        gf = nat_c[:, :, :].rearrange("p a b -> p (a b)")

        pair = [ctx.enter_context(nc.psum_tensor(f"pair{i}", [P, 2, 512], F32)) for i in range(2)]
        bank = [ctx.enter_context(nc.psum_tensor(f"bank{i}", [P, 512], F32)) for i in range(4, 8)]
        p_logits, p_moba, p_ret, p_retv = bank

        x_loaded = [sem(f"x_loaded{t}") for t in range(2)]
        first_half = sem("first_half")
        zeros_made = sem("zeros_made")
        g1_loaded = sem("g1_loaded")
        ident_loaded = sem("ident_loaded")
        rows_loaded = sem("rows_loaded")
        consts_loaded = sem("consts_loaded")
        x_again = sem("x_again")
        gf_loaded = sem("gf_loaded")
        w_loaded = [sem(f"w_loaded{i}") for i in range(SLOTS)]
        hi_made = sem("hi_made")
        lo_made = sem("lo_made")
        first_hi = sem("first_hi")
        first_lo = sem("first_lo")
        units_used = sem("units_used")
        half_made = sem("half_made")
        out_read = sem("out_read")
        side_made = sem("side_made")
        const_half = sem("const_half")
        sq_made = sem("sq_made")
        ms_made = sem("ms_made")
        rstd_made = sem("rstd_made")
        h_made = sem("h_made")
        cols_t = sem("cols_t")
        cols_made = sem("cols_made")
        xt_made = sem("xt_made")
        xt_hi = sem("xt_hi")
        xt_lo = sem("xt_lo")
        rg_sig = sem("rg_sig")
        dve_step = sem("dve_step")
        act_step = sem("act_step")
        logits_made = sem("logits_made")
        logits_read = sem("logits_read")
        top_made = sem("top_made")
        probs_made = sem("probs_made")
        probs_normed = sem("probs_normed")
        pt_made = sem("pt_made")
        pt_read = sem("pt_read")
        moba_made = sem("moba_made")
        moba_read = sem("moba_read")
        mt_hi = sem("mt_hi")
        mt_lo = sem("mt_lo")
        rs_made = sem("rs_made")
        rs_read = sem("rs_read")
        rv_made = sem("rv_made")
        ret_sq = sem("ret_sq")
        ret_ms = sem("ret_ms")
        ret_rstd = sem("ret_rstd")
        ret_done = sem("ret_done")
        rt_made = sem("rt_made")
        rt_hi = sem("rt_hi")
        rt_lo = sem("rt_lo")
        gate_sig = sem("gate_sig")
        gated_made = sem("gated_made")
        merged_made = sem("merged_made")
        merged_hi = sem("merged_hi")
        merged_lo = sem("merged_lo")
        x2_made = sem("x2_made")
        x2_sq = sem("x2_sq")
        hid_made = sem("hid_made")
        hid_hi = sem("hid_hi")
        hid_lo = sem("hid_lo")
        down_made = sem("down_made")
        x3_made = sem("x3_made")
        x3_sq = sem("x3_sq")
        x3_ms = sem("x3_ms")
        x3_rstd = sem("x3_rstd")
        x3_gained = sem("x3_gained")
        y_made = sem("y_made")
        y_stored = sem("y_stored")

        def unit_source(u):
            if u < U_NAT:
                c = 256 * u + (2048 if u >= 4 else 0)
                return w_in_v[:, :, c:c + 256]
            if u < U_GATE:
                n, half = divmod(u - U_NAT, 2)
                c = [2048, 2560, 1024, 1536, 4096][n]
                return w_in_v[:, 4 * half:4 * half + 4, c:c + 512]
            if u < U_RET:
                c = 4608 + 256 * (u - U_GATE)
                return w_in_v[:, :, c:c + 256]
            if u < U_MOBA:
                c = 256 * (u - U_RET)
                return w_ret_v[:, :, c:c + 256]
            if u < U_OUT:
                c = 512 * (u - U_MOBA)
                return w_moba_v[:, :, c:c + 512]
            half, n = divmod(u - U_OUT, 2)
            return w_out_v[:, 4 * half:4 * half + 4, 512 * n:512 * n + 512]

        def unit(u):
            return u % SLOTS, u // SLOTS

        def output_wait(eng, o):
            if o < O_NAT:
                eng.wait_ge(units_used, o + 1)
            elif o < O_GATE:
                eng.wait_ge(units_used, U_NAT + 2 * (o - O_NAT) + 2)
            elif o < O_MOBA:
                eng.wait_ge(units_used, U_GATE + o - O_GATE + 1)
            elif o < O_OUT and (o - O_MOBA) % 2 == 0:
                eng.wait_ge(half_made, (o - O_MOBA) // 2 + 1)
            elif o < O_OUT:
                eng.wait_ge(units_used, U_MOBA + (o - O_MOBA) // 2 + 1)
            else:
                eng.wait_ge(units_used, U_OUT + 3 + o - O_OUT)

        def x_bank(k):
            return bank[k % 4][:, (k // 4) * T:(k // 4) * T + T]

        def wide(ring, slot):
            return ring[:, slot, :].rearrange("p (k n) -> p k n", k=8)

        def mid(ring, slot):
            return ring[:, slot, :].rearrange("p (k n) -> p k n", k=4)

        def long(ring, slot):
            return ring[:, slot, :].rearrange("p (k n) -> p k n", k=2)

        block = ctx.enter_context(nc.Block())

        @block.sync
        def _(sp):
            def load(slot, rnd, view, source):
                if type(rnd) is not int or rnd > 0:
                    sp.wait_ge(lo_made, SLOTS * (rnd - 1) + slot + 1)
                sp.dma_start(view(w_raw, slot), source).then_inc(w_loaded[slot], 16)

            def load_before_mlp(u):
                view = mid if U_NAT <= u < U_GATE or u >= U_MOBA else wide
                load(u % SLOTS, u // SLOTS, view, unit_source(u))

            def load_up(kind, c, half):
                load(kind[0], kind[1] + c, wide, w_up_v[:, :, bass.ds(512 * (c + 1) + 256 * half, 256)])

            def load_down(kind, c, half):
                load(kind[0], kind[1] + c, long, w_down_v[:, bass.ds(4 * c + 2 * half, 2), :])

            for t in range(2):
                sp.dma_start(nat_b[:, t, :], x_v[:, t, :]).then_inc(x_loaded[t], 16)
            sp.dma_start(g1_rows[:, :], norm1_g.rearrange("a (k p) -> (a k) p", p=P)).then_inc(g1_loaded, 16)
            sp.dma_start(wide(w_raw, 0)[:, 0:4, :], unit_source(0)[:, 0:4, :]).then_inc(first_half, 16)
            sp.dma_start(wide(w_raw, 0)[:, 4:8, :], unit_source(0)[:, 4:8, :]).then_inc(w_loaded[0], 16)
            for u in range(1, SLOTS):
                load_before_mlp(u)
            sp.dma_start(rows[0:8, :], norm2_g.rearrange("a (k p) -> (a k) p", p=P)).then_inc(rows_loaded, 16)
            sp.dma_start(rows[8:24, :], b_gate.rearrange("a (k p) -> (a k) p", p=P)).then_inc(rows_loaded, 16)
            sp.dma_start(decay[:, :, :], consts[:, P:P + RET_SCALE_COLS].rearrange("p (h t) -> p h t", h=RET_HEADS)
                         ).then_inc(consts_loaded, 16)
            sp.dma_start(distance[:, :], consts[:, P + RET_SCALE_COLS:]).then_inc(consts_loaded, 16)
            for u in range(SLOTS, U_OUT):
                load_before_mlp(u)
            sp.wait_ge(rv_made, RET_HEADS)
            sp.dma_start(nat_b[:, :, :], x_v).then_inc(x_again, 16)
            sp.wait_ge(moba_made, MOBA_HEADS)
            sp.dma_start(gf, normf_g.rearrange("(a d) -> a d", a=1).to_broadcast([P, D])).then_inc(gf_loaded, 16)
            for u in range(U_OUT, U_MLP):
                load_before_mlp(u)
            load(0, 9, wide, w_up_v[:, :, 0:256])
            load(1, 9, wide, w_up_v[:, :, 256:512])
            with sp.Fori(0, MLP_CHUNKS - 1) as c:
                load_down(DOWN_A, c, 0)
                load_up(UP_A, c, 0)
                load_down(DOWN_B, c, 1)
                load_up(UP_B, c, 1)
            load(2, 16, long, w_down_v[:, 28:30, :])
            load(3, 16, long, w_down_v[:, 30:32, :])
            for t in range(2):
                for n in range(2):
                    sp.wait_ge(y_made, 2 * t + n + 1)
                    sp.dma_start(out_v[:, t, 512 * n:512 * n + 512], nat_b[:, t, 512 * n:512 * n + 512]
                                 ).then_inc(y_stored, 16)
            sp.wait_ge(y_stored, 64)

        @block.gpsimd
        def _(pool):
            pool.dma_start(ident[:, :], consts[:, 0:P]).then_inc(ident_loaded, 16)
            nc.gpsimd.memset(neg_half[:, :], -0.5).then_inc(const_half, 1)
            pool.wait_ge(const_half, 1)

            def power(wanted, count, source, made, width):
                pool.wait_ge(wanted, count)
                nc.gpsimd.tensor_tensor(rstd[:, source:source + width], ms[:, source:source + width],
                                        neg_half[:, 0:width], ALU.pow).then_inc(made, 1)

            for t in range(2):
                power(ms_made, t + 1, t, rstd_made, 1)
            for h in range(RET_HEADS):
                if h:
                    pool.wait_ge(ret_done, h)
                power(ret_ms, h + 1, 2, ret_rstd, 2)
            for m in range(4):
                pool.wait_ge(gated_made, 4 + m + 1)
                if m >= 2:
                    pool.wait_ge(merged_lo, m - 1)
                nc.gpsimd.tensor_tensor(merged[:, m % 2, :, :], gates[:, 2 * m:2 * m + 2, :],
                                        gates[:, 8 + 2 * m:10 + 2 * m, :], ALU.add).then_inc(merged_made, 1)
            for t in range(2):
                power(x3_ms, t + 1, 6 + t, x3_rstd, 1)

        @block.scalar
        def _(act):
            def make_hi(slot, rnd):
                act.wait_ge(w_loaded[slot], 16 * rnd + 16)
                if type(rnd) is not int or rnd > 0:
                    act.wait_ge(units_used, SLOTS * (rnd - 1) + slot + 1)
                nc.scalar.copy(w_hi[:, slot, :], w_raw[:, slot, :]).then_inc(hi_made, 1)

            def make_side(o):
                output_wait(act, o)
                if o > 0:
                    act.wait_ge(out_read, o)
                nc.scalar.copy(side[:, :, :], pair[o % 2][:, :, T:]).then_inc(side_made, 1)

            act.wait_ge(x_loaded[0], 16)
            nc.scalar.activation(junk, nat_b[:, 0, :], ACT.Square, accum_out=sq[:, 0:1]).then_inc(sq_made, 1)
            act.wait_ge(x_loaded[1], 16)
            act.wait_ge(sq_made, 1)
            nc.scalar.activation(junk, nat_b[:, 1, :], ACT.Square, accum_out=sq[:, 1:2]).then_inc(sq_made, 1)
            act.wait_ge(first_half, 16)
            nc.scalar.copy(w_hi[:, 0, 0:UNIT // 2], w_raw[:, 0, 0:UNIT // 2]).then_inc(first_hi, 1)
            act.wait_ge(cols_made, 1)
            for k in range(KD):
                act.wait_ge(xt_made, k + 5 if k < 4 else KD)
                if k >= 4:
                    act.wait_ge(xt_lo, k - 3)
                nc.scalar.activation(act_a[:, k, 0, :], x_bank(k), ACT.Copy,
                                     scale=cols[:, k:k + 1]).then_inc(xt_hi, 1)
                if k == 3:
                    act.wait_ge(w_loaded[0], 16)
                    nc.scalar.copy(w_hi[:, 0, UNIT // 2:], w_raw[:, 0, UNIT // 2:]).then_inc(hi_made, 1)
            make_hi(1, 0)
            make_hi(2, 0)

            for u in range(U_QK, U_NAT):
                if u > 0:
                    make_side(O_QK + u - 1)
                make_hi(*unit(u + AHEAD))
            for u in range(U_NAT, U_GATE):
                if u == U_NAT:
                    make_side(O_NAT - 1)
                if u in (U_NAT + 2, U_NAT + 4):
                    n = (u - U_NAT) // 2 - 1
                    output_wait(act, O_NAT + n)
                    nc.scalar.activation(nat_a[:, :, 512 * n:512 * n + 512], pair[(O_NAT + n) % 2][:, :, :],
                                         ACT.Sigmoid).then_inc(rg_sig, 1)
                make_hi(*unit(u + AHEAD))

            def softmax(h):
                act.wait_ge(top_made, h + 1)
                if h:
                    act.wait_ge(probs_normed, 2 * h)
                for t, (a, b) in enumerate(((0, P), (P, 3 * P))):
                    nc.scalar.activation(scratch[:, a:b], scratch[:, a:b], ACT.Exp, bias=neg_top[:, t:t + 1],
                                         scale=MOBA_DIM ** -0.5, accum_out=prob_sum[:, t:t + 1]
                                         ).then_inc(probs_made, 1)

            def probs_out(h):
                act.wait_ge(pt_made, h + 1)
                if h:
                    act.wait_ge(moba_made, h)
                nc.scalar.copy(probs_t[:, :], p_moba[:, 0:3 * P]).then_inc(pt_read, 1)

            def ret_squares(j):
                act.wait_ge(rv_made, j + 1)
                if j:
                    act.wait_ge(ret_ms, j)
                for t in range(2):
                    if j or t:
                        act.wait_ge(ret_sq, 2 * j + t)
                    nc.scalar.activation(ret_junk[:, :], p_retv[:, t * RET_V:(t + 1) * RET_V], ACT.Square,
                                         accum_out=sq[:, 2 + t:3 + t]).then_inc(ret_sq, 1)

            def ret_hi(j):
                act.wait_ge(rt_made, j + 1)
                nc.scalar.copy(act_b[:, 2 * j:2 * j + 2, 0, :], p_retv[:, :].rearrange("p (k t) -> p k t", k=2)
                               ).then_inc(rt_hi, 1)

            def moba_copy(h):
                a = (h % 2) * MOBA_DIM
                act.wait_ge(moba_made, h + 1)
                if h >= 2 and h % 2 == 0:
                    act.wait_ge(mt_lo, h // 2)
                nc.scalar.copy(moba_out[a:a + MOBA_DIM, :], p_moba[a:a + MOBA_DIM, 0:T]).then_inc(moba_read, 1)

            def moba_hi(p):
                act.wait_ge(moba_read, 2 * p + 2)
                nc.scalar.copy(act_c[:, p, 0, :], moba_out[:, :]).then_inc(mt_hi, 1)

            softmax(0)
            for i in range(MOBA_HEADS):
                u = U_GATE + i
                if i > 0:
                    moba_copy(i - 1)
                    make_side(O_GATE + i - 1)
                    if i % 2 == 0:
                        moba_hi(i // 2 - 1)
                probs_out(i)
                if i + 1 < MOBA_HEADS:
                    make_hi(*unit(u + AHEAD))
                    softmax(i + 1)
                if i % 2 == 0:
                    ret_squares(i // 2)
                else:
                    ret_hi(i // 2)
            moba_copy(MOBA_HEADS - 1)
            for u in range(U_RET, U_MOBA):
                o = u - 1 - U_RET + O_RET
                if u == U_RET:
                    make_side(O_RET - 1)
                    moba_hi(3)
                    make_hi(*unit(U_RET - 1 + AHEAD))
                    act.wait_ge(out_read, O_RET)
                    act.wait_ge(cols_made, 2)
                    for g in range(8):
                        nc.scalar.activation(gates[:, g, :], gates[:, g, :], ACT.Sigmoid,
                                             bias=cols[:, 16 + g:17 + g]).then_inc(gate_sig, 1)
                else:
                    make_side(o)
                make_hi(*unit(u + AHEAD))
                if u == U_RET + 1:
                    for g in range(8, 16):
                        nc.scalar.activation(gates[:, g, :], gates[:, g, :], ACT.Sigmoid,
                                             bias=cols[:, 16 + g:17 + g]).then_inc(gate_sig, 1)

            def merged_out(m):
                act.wait_ge(merged_made, m + 1)
                nc.scalar.copy(act_a[:, 2 * m:2 * m + 2, 0, :], merged[:, m % 2, :, :]).then_inc(merged_hi, 1)

            make_side(O_RET + 3)
            make_side(O_MOBA)
            make_hi(*unit(U_MOBA + AHEAD))
            for m in range(4):
                if m < 3:
                    make_side(O_MOBA + m + 1)
                merged_out(m)

            def x2_squares(n):
                for t in range(2):
                    act.wait_ge(x2_made, 2 * n + t + 1)
                    if n or t:
                        act.wait_ge(x2_sq, 2 * n + t)
                    nc.scalar.activation(junk[:, 0:512], nat_b[:, t, 512 * n:512 * n + 512], ACT.Square,
                                         accum_out=sq[:, 4 + 2 * n + t:5 + 2 * n + t]).then_inc(x2_sq, 1)

            def x2_hi(n):
                for k in range(4 * n, 4 * n + 4):
                    act.wait_ge(xt_made, KD + k + 1)
                    nc.scalar.activation(act_b[:, k, 0, :], x_bank(k), ACT.Copy,
                                         scale=cols[:, 8 + k:9 + k]).then_inc(xt_hi, 1)

            for u in range(U_OUT - 1, U_OUT + 3):
                make_hi(*unit(u + AHEAD))
            x2_hi(0)
            x2_hi(1)
            make_hi(*unit(U_OUT + 3 + AHEAD))

            def hidden_out(n, half):
                act.wait_ge(hid_made, n + 1)
                nc.scalar.copy(act_c[:, 2 * half:2 * half + 2, 0, :], up_sqr).then_inc(hid_hi, 1)

            def up_side(used, n, half):
                act.wait_ge(units_used, used)
                act.wait_ge(out_read, O_OUT + n)
                nc.scalar.copy(side[:, :, :], pair[(O_UP + half) % 2][:, :, T:]).then_inc(side_made, 1)

            up_side(U_MLP + 1, 0, 0)
            hidden_out(0, 0)
            make_hi(*unit(U_MLP + AHEAD))
            make_hi(*unit(U_MLP + 1 + AHEAD))

            def mlp_slots(c, last):
                up_side(38 + 4 * c, 2 * c + 1, 1)
                make_hi(UP_B[0], UP_B[1] + c)
                act.wait_ge(units_used, 37 + 4 * c)
                hidden_out(2 * c + 1, 1)
                make_hi(DOWN_A[0], DOWN_A[1] + 1 + c)
                up_side(40 + 4 * c, 2 * c + 2, 0)
                make_hi(UP_A[0], UP_A[1] + 1 + c)
                act.wait_ge(units_used, 39 + 4 * c)
                hidden_out(2 * c + 2, 0)
                if not last:
                    make_hi(DOWN_B[0], DOWN_B[1] + 1 + c)

            with act.Fori(0, MLP_CHUNKS - 2) as c:
                mlp_slots(c, False)
            mlp_slots(MLP_CHUNKS - 2, True)
            up_side(38 + 4 * (MLP_CHUNKS - 1), 2 * MLP_CHUNKS - 1, 1)
            act.wait_ge(units_used, 37 + 4 * (MLP_CHUNKS - 1))
            hidden_out(2 * MLP_CHUNKS - 1, 1)
            x2_squares(0)
            x2_squares(1)
            for t in range(2):
                for n in range(2):
                    act.wait_ge(x3_made, 2 * t + n + 1)
                    if t or n:
                        act.wait_ge(x3_sq, 2 * t + n)
                    nc.scalar.activation(junk[:, 0:512], nat_a[:, t, 512 * n:512 * n + 512], ACT.Square,
                                         accum_out=sq[:, 2 * t + n:2 * t + n + 1]).then_inc(x3_sq, 1)

        @block.vector
        def _(dve):
            steps = [0]

            def link(ins):
                steps[0] += 1
                ins.then_inc(dve_step, 1)
                dve.wait_ge(dve_step, steps[0])

            def make_lo(slot, rnd):
                dve.wait_ge(hi_made, SLOTS * rnd + slot + 1)
                nc.vector.tensor_tensor(w_lo[:, slot, :], w_raw[:, slot, :], w_hi[:, slot, :].bitcast(F32),
                                        ALU.subtract).then_inc(lo_made, 1)

            def add_side(o, s, parity, into):
                dve.wait_ge(side_made, s + 1)
                nc.vector.tensor_tensor(into, pair[parity][:, :, 0:T], side[:, :, :], ALU.add).then_inc(out_read, 1)

            nc.vector.memset(zeros[:, :], 0.0).then_inc(zeros_made, 1)

            def mean_square(t):
                nc.vector.tensor_scalar(ms[:, t:t + 1], sq[:, t:t + 1], 1.0 / D, EPS, ALU.mult, ALU.add
                                        ).then_inc(ms_made, 1)

            def normed(t):
                dve.wait_ge(rstd_made, t + 1)
                nc.vector.tensor_scalar(nat_a[:, t, :], nat_b[:, t, :], rstd[:, t:t + 1], None, ALU.mult
                                        ).then_inc(h_made, 1)

            for t in range(2):
                dve.wait_ge(sq_made, t + 1)
                mean_square(t)
                normed(t)
            dve.wait_ge(cols_t, 1)
            nc.vector.tensor_copy(cols[:, 0:8], pair[1][:, 0, 0:8]).then_inc(cols_made, 1)
            dve.wait_ge(first_hi, 1)
            nc.vector.tensor_tensor(w_lo[:, 0, 0:UNIT // 2], w_raw[:, 0, 0:UNIT // 2],
                                    w_hi[:, 0, 0:UNIT // 2].bitcast(F32), ALU.subtract).then_inc(first_lo, 1)
            dve.wait_ge(cols_made, 1)
            for k in range(KD):
                dve.wait_ge(xt_hi, k + 1)
                nc.vector.scalar_tensor_tensor(out=act_a[:, k, 1, :], in0=x_bank(k),
                                               scalar=cols[:, k:k + 1], in1=act_a[:, k, 0, :].bitcast(F32),
                                               op0=ALU.mult, op1=ALU.subtract).then_inc(xt_lo, 1)
                if k == 3:
                    dve.wait_ge(hi_made, 1)
                    nc.vector.tensor_tensor(w_lo[:, 0, UNIT // 2:], w_raw[:, 0, UNIT // 2:],
                                            w_hi[:, 0, UNIT // 2:].bitcast(F32), ALU.subtract).then_inc(lo_made, 1)
            make_lo(1, 0)
            make_lo(2, 0)

            for u in range(U_QK, U_NAT):
                if u > 0:
                    add_side(O_QK + u - 1, S_QK + u - 1, (u - 1) % 2, qk[:, 2 * u - 2:2 * u, :])
                make_lo(*unit(u + AHEAD))

            def natural_out(n):
                o = O_NAT + n
                source = pair[o % 2][:, :, :]
                if n < 2:
                    part = nat_a[:, :, 512 * n:512 * n + 512]
                    dve.wait_ge(rg_sig, n + 1)
                    nc.vector.tensor_tensor(part, source, part, ALU.mult).then_inc(out_read, 1)
                    return
                output_wait(dve, o)
                if n < 4:
                    nc.vector.tensor_copy(nat_b[:, :, 512 * (n - 2):512 * (n - 2) + 512], source).then_inc(out_read, 1)
                else:
                    nc.vector.tensor_copy(nat_c[:, :, :], source).then_inc(out_read, 1)

            for u in range(U_NAT, U_GATE):
                if u == U_NAT:
                    add_side(O_NAT - 1, S_GATE - 1, 1, qk[:, 14:16, :])
                elif (u - U_NAT) % 2 == 0:
                    natural_out((u - U_NAT) // 2 - 1)
                make_lo(*unit(u + AHEAD))

            def logits(h):
                dve.wait_ge(logits_made, h + 1)
                if h == 0:
                    dve.wait_ge(consts_loaded, 32)
                else:
                    dve.wait_ge(pt_made, h)
                slope = 2.0 ** -(h + 1)
                nc.vector.scalar_tensor_tensor(out=scratch[:, :], in0=distance[:, :], scalar=-slope * MOBA_DIM ** 0.5,
                                               in1=p_logits[:, 0:3 * P], op0=ALU.mult, op1=ALU.add
                                               ).then_inc(logits_read, 1)
                dve.wait_ge(logits_read, h + 1)
                nc.vector.reduce_max(top[:, 0:1], scratch[:, 0:P], AX_X).then_inc(dve_step, 1)
                steps[0] += 1
                link(nc.vector.reduce_max(top[:, 1:2], scratch[:, P:3 * P], AX_X))
                nc.vector.tensor_scalar(neg_top[:, :], top[:, 0:2], -MOBA_DIM ** -0.5, None, ALU.mult
                                        ).then_inc(top_made, 1)

            def decayed(j):
                dve.wait_ge(rs_made, j + 1)
                if j:
                    dve.wait_ge(rv_made, j)
                for a, b in ((0, T), (T, T + P)):
                    nc.vector.tensor_tensor(ret_scores[:, a:b], p_ret[:, a:b], decay[:, j, 0:b - a], ALU.mult
                                            ).then_inc(rs_read, 1)

            def probs_norm(h):
                dve.wait_ge(probs_made, 2 * h + 2)
                link(nc.vector.reciprocal(prob_inv[:, :], prob_sum[:, :]))
                for t, (a, b) in enumerate(((0, P), (P, 3 * P))):
                    nc.vector.tensor_scalar(scratch[:, a:b], scratch[:, a:b], prob_inv[:, t:t + 1], None, ALU.mult
                                            ).then_inc(probs_normed, 1)

            def ret_norm(j):
                dve.wait_ge(ret_sq, 2 * j + 2)
                nc.vector.tensor_scalar(ms[:, 2:4], sq[:, 2:4], 1.0 / RET_V, EPS, ALU.mult, ALU.add
                                        ).then_inc(ret_ms, 1)
                dve.wait_ge(ret_rstd, j + 1)
                for t in range(2):
                    part = nat_a[:, t, j * RET_V:(j + 1) * RET_V]
                    ins = nc.vector.scalar_tensor_tensor(out=part, in0=p_retv[:, t * RET_V:(t + 1) * RET_V],
                                                         scalar=rstd[:, 2 + t:3 + t], in1=part,
                                                         op0=ALU.mult, op1=ALU.mult)
                    if t == 0:
                        link(ins)
                    else:
                        ins.then_inc(ret_done, 1)

            def ret_lo(j):
                dve.wait_ge(rt_hi, j + 1)
                nc.vector.tensor_tensor(act_b[:, 2 * j:2 * j + 2, 1, :], p_retv[:, :].rearrange("p (k t) -> p k t", k=2),
                                        act_b[:, 2 * j:2 * j + 2, 0, :].bitcast(F32), ALU.subtract).then_inc(rt_lo, 1)

            def moba_lo(p):
                dve.wait_ge(mt_hi, p + 1)
                nc.vector.tensor_tensor(act_c[:, p, 1, :], moba_out[:, :], act_c[:, p, 0, :].bitcast(F32),
                                        ALU.subtract).then_inc(mt_lo, 1)

            dve.wait_ge(cols_t, 2)
            nc.vector.tensor_copy(cols[:, 8:32], p_retv[:, 0:24]).then_inc(cols_made, 1)
            logits(0)
            decayed(0)
            natural_out(4)
            probs_norm(0)
            for i in range(MOBA_HEADS):
                u = U_GATE + i
                if i > 0:
                    o = O_GATE + i - 1
                    add_side(o, S_GATE + i - 1, o % 2, gates[:, 2 * i - 2:2 * i, :])
                    if i % 2 == 0:
                        decayed(i // 2)
                        moba_lo(i // 2 - 1)
                if i + 1 < MOBA_HEADS:
                    logits(i + 1)
                    make_lo(*unit(u + AHEAD))
                    probs_norm(i + 1)
                if i % 2 == 0:
                    ret_norm(i // 2)
                else:
                    ret_lo(i // 2)

            gated_count = [0]

            def gated(o, pair_of_tiles, first_gate):
                n = pair_of_tiles
                add_side(o, S_RET + o - O_RET, o % 2, branch)
                dve.wait_ge(out_read, o + 1)
                g = gates[:, first_gate + 2 * n:first_gate + 2 * n + 2, :]
                dve.wait_ge(gate_sig, first_gate + 2 * n + 2)
                nc.vector.tensor_tensor(g, branch, g, ALU.mult).then_inc(gated_made, 1)
                gated_count[0] += 1
                dve.wait_ge(gated_made, gated_count[0])

            for u in range(U_RET, U_MOBA):
                if u == U_RET:
                    o = O_RET - 1
                    add_side(o, S_RET - 1, o % 2, gates[:, 14:16, :])
                    moba_lo(3)
                    make_lo(*unit(U_RET - 1 + AHEAD))
                else:
                    gated(u - 1 - U_RET + O_RET, u - 1 - U_RET, 0)
                make_lo(*unit(u + AHEAD))

            def merged_lo_of(m):
                dve.wait_ge(merged_hi, m + 1)
                nc.vector.tensor_tensor(act_a[:, 2 * m:2 * m + 2, 1, :], merged[:, m % 2, :, :],
                                        act_a[:, 2 * m:2 * m + 2, 0, :].bitcast(F32), ALU.subtract
                                        ).then_inc(merged_lo, 1)

            gated(O_RET + 3, 3, 0)
            gated(O_MOBA, 0, 8)
            make_lo(*unit(U_MOBA + AHEAD))
            for m in range(4):
                if m < 3:
                    gated(O_MOBA + m + 1, m + 1, 8)
                merged_lo_of(m)

            def residual(n):
                o = O_OUT + n
                if n == 0:
                    dve.wait_ge(x_again, 16)
                output_wait(dve, o)
                for t in range(2):
                    part = nat_b[:, t, 512 * n:512 * n + 512]
                    nc.vector.tensor_tensor(part, pair[o % 2][:, t, :], part, ALU.add).then_inc(x2_made, 1)

            def x2_lo(n):
                for k in range(4 * n, 4 * n + 4):
                    dve.wait_ge(xt_hi, KD + k + 1)
                    nc.vector.scalar_tensor_tensor(out=act_b[:, k, 1, :],
                                                   in0=x_bank(k),
                                                   scalar=cols[:, 8 + k:9 + k], in1=act_b[:, k, 0, :].bitcast(F32),
                                                   op0=ALU.mult, op1=ALU.subtract).then_inc(xt_lo, 1)

            for u in range(U_OUT - 1, U_OUT + 3):
                make_lo(*unit(u + AHEAD))
                if u == U_OUT + 1:
                    residual(0)
            x2_lo(0)
            residual(1)
            x2_lo(1)
            make_lo(*unit(U_OUT + 3 + AHEAD))

            def hidden_sum(n, half):
                add_side(None, S_UP + n, (O_UP + half) % 2, up_sum)
                dve.wait_ge(out_read, O_OUT + n + 1)
                nc.vector.scalar_tensor_tensor(out=up_sqr, in0=up_sum, scalar=0.0, in1=up_sum,
                                               op0=ALU.max, op1=ALU.mult).then_inc(hid_made, 1)

            def hidden_lo(n, half):
                dve.wait_ge(hid_hi, n + 1)
                nc.vector.tensor_tensor(act_c[:, 2 * half:2 * half + 2, 1, :], up_sqr,
                                        act_c[:, 2 * half:2 * half + 2, 0, :].bitcast(F32), ALU.subtract
                                        ).then_inc(hid_lo, 1)

            hidden_sum(0, 0)
            hidden_lo(0, 0)
            make_lo(*unit(U_MLP + AHEAD))
            make_lo(*unit(U_MLP + 1 + AHEAD))

            def mlp_slots(c, last):
                dve.wait_ge(hid_lo, 2 * c + 1)
                hidden_sum(2 * c + 1, 1)
                make_lo(UP_B[0], UP_B[1] + c)
                hidden_lo(2 * c + 1, 1)
                make_lo(DOWN_A[0], DOWN_A[1] + 1 + c)
                dve.wait_ge(hid_lo, 2 * c + 2)
                hidden_sum(2 * c + 2, 0)
                make_lo(UP_A[0], UP_A[1] + 1 + c)
                hidden_lo(2 * c + 2, 0)
                if not last:
                    make_lo(DOWN_B[0], DOWN_B[1] + 1 + c)

            with dve.Fori(0, MLP_CHUNKS - 2) as c:
                mlp_slots(c, False)
            mlp_slots(MLP_CHUNKS - 2, True)
            dve.wait_ge(hid_lo, 2 * MLP_CHUNKS - 1)
            hidden_sum(2 * MLP_CHUNKS - 1, 1)
            hidden_lo(2 * MLP_CHUNKS - 1, 1)

            dve.wait_ge(x2_sq, 4)
            link(nc.vector.tensor_tensor(ms[:, 4:6], sq[:, 4:6], sq[:, 6:8], ALU.add))
            link(nc.vector.tensor_scalar(ms[:, 4:6], ms[:, 4:6], 1.0 / D, EPS, ALU.mult, ALU.add))
            link(nc.vector.reciprocal(rstd[:, 4:6], ms[:, 4:6]))
            dve.wait_ge(gf_loaded, 16)
            def x3(t, n):
                dve.wait_ge(down_made, 2 * t + n + 1)
                part = slice(512 * n, 512 * n + 512)
                nc.vector.scalar_tensor_tensor(out=nat_a[:, t, part], in0=bank[2 * t + n][:, :],
                                               scalar=rstd[:, 4 + t:5 + t], in1=nat_b[:, t, part],
                                               op0=ALU.mult, op1=ALU.add).then_inc(x3_made, 1)

            def gained(t):
                for n in range(2):
                    part = slice(512 * n, 512 * n + 512)
                    dve.wait_ge(x3_made, 2 * t + n + 1)
                    nc.vector.tensor_tensor(nat_b[:, t, part], nat_a[:, t, part], gf[:, part], ALU.mult
                                            ).then_inc(x3_gained, 1)

            def mean(t):
                dve.wait_ge(x3_sq, 2 * t + 1)
                link(nc.vector.tensor_scalar(ms[:, 6 + t:7 + t], sq[:, 2 * t:2 * t + 1], 1.0 / D, EPS,
                                             ALU.mult, ALU.add))
                dve.wait_ge(x3_sq, 2 * t + 2)
                nc.vector.scalar_tensor_tensor(out=ms[:, 6 + t:7 + t], in0=sq[:, 2 * t + 1:2 * t + 2], scalar=1.0 / D,
                                               in1=ms[:, 6 + t:7 + t], op0=ALU.mult, op1=ALU.add).then_inc(x3_ms, 1)

            def normed_out(t):
                dve.wait_ge(x3_rstd, t + 1)
                dve.wait_ge(x3_gained, 2 * t + 2)
                for n in range(2):
                    part = nat_b[:, t, 512 * n:512 * n + 512]
                    nc.vector.tensor_scalar(part, part, rstd[:, 6 + t:7 + t], None, ALU.mult).then_inc(y_made, 1)

            x3(0, 0)
            x3(0, 1)
            gained(0)
            mean(0)
            x3(1, 0)
            normed_out(0)
            x3(1, 1)
            gained(1)
            mean(1)
            normed_out(1)

        @block.tensor
        def _(pe):
            def transposed(view_hi, view_lo, moving, col, into, ready=None, tiles=None):
                k_tiles = view_hi.shape[1]
                for k in tiles or range(k_tiles):
                    if ready:
                        made, before, per = ready
                        if k % per == 0:
                            pe.wait_ge(made, before + k // per + 1)
                    whole = (into[:, :], view_hi[:, k, col:col + P], moving[:, k, :, :])
                    left = (into[:, 0:T], view_lo[:, k, col:col + P], moving[:, k, 0, :])
                    if k < k_tiles - 1:
                        nc.tensor.matmul(*whole, start=(k == 0), stop=False)
                        ins = nc.tensor.matmul(*left, start=False, stop=False)
                    else:
                        nc.tensor.matmul(*left, start=False, stop=False)
                        ins = nc.tensor.matmul(*whole, start=False, stop=True)
                return ins

            def unit_ready(slot, rnd):
                pe.wait_ge(lo_made, SLOTS * rnd + slot + 1)

            def output_free(o):
                if o >= 2:
                    pe.wait_ge(out_read, o - 1)

            def half_wide(slot, moving, parity, n, ready=None, tiles=None):
                return transposed(wide(w_hi, slot), wide(w_lo, slot), moving, n * P, pair[parity][:, n, :],
                                  ready, tiles)

            def wide_unit(slot, rnd, moving, parity, ready=None):
                unit_ready(slot, rnd)
                half_wide(slot, moving, parity, 0, ready)
                half_wide(slot, moving, parity, 1).then_inc(units_used, 1)

            def natural_unit(u, moving, parity, half, between=None):
                slot = u % SLOTS
                unit_ready(*unit(u))
                hi, lo = mid(w_hi, slot), mid(w_lo, slot)
                for t in range(2):
                    for k in range(4):
                        for n, (part, w) in enumerate(((0, hi), (0, lo), (1, hi))):
                            ins = nc.tensor.matmul(pair[parity][:, t, :],
                                                   moving[:, 4 * half + k, part, t * P:(t + 1) * P], w[:, k, :],
                                                   start=(half == 0 and k == 0 and n == 0),
                                                   stop=(half == 1 and k == 3 and n == 2))
                    if t == 0 and between:
                        between()
                ins.then_inc(units_used, 1)

            pe.wait_ge(zeros_made, 1)
            for i in range(WARM_UP):
                nc.tensor.matmul(p_logits[:, 0:T], zeros[:, 0:P], zeros[:, :], start=True, stop=True)
            pe.wait_ge(ident_loaded, 16)
            pe.wait_ge(g1_loaded, 16)
            nc.tensor.transpose(pair[1][:, 0, 0:8], g1_rows[:, :], ident[0:8, 0:8]).then_inc(cols_t, 1)
            for t in range(2):
                pe.wait_ge(h_made, t + 1)
                for k in range(KD):
                    ins = nc.tensor.transpose(x_bank(k)[:, t * P:(t + 1) * P],
                                              nat_a[:, t, k * P:(k + 1) * P], ident[:, :])
                    if t == 1:
                        ins.then_inc(xt_made, 1)

            for part in range(2):
                if part == 0:
                    pe.wait_ge(first_lo, 1)
                else:
                    unit_ready(0, 0)
                for n in range(2):
                    ins = half_wide(0, act_a, 0, n, (xt_lo, 0, 1), range(4 * part, 4 * part + 4))
            ins.then_inc(units_used, 1)
            pe.wait_ge(cols_made, 1)
            for u in range(U_QK + 1, U_NAT):
                o = O_QK + u
                output_free(o)
                wide_unit(*unit(u), act_a, o % 2)
            def first_scores():
                pe.wait_ge(out_read, O_QK + 8)
                pe.wait_ge(xt_lo, KD)
                pe.wait_ge(rows_loaded, 32)
                nc.tensor.transpose(p_retv[:, 0:24], rows[:, :], ident[0:24, 0:24]).then_inc(cols_t, 1)
                moba_scores(0)
                ret_scores_of(0)

            def moba_scores(h):
                if h:
                    pe.wait_ge(logits_read, h)
                a, q, k = (h % 2) * MOBA_DIM, 8 + h // 2, 12 + h // 2
                nc.tensor.matmul(p_logits[:, 0:P], qk[a:a + MOBA_DIM, q, 0:P], qk[a:a + MOBA_DIM, k, 0:P],
                                 start=True, stop=True)
                nc.tensor.matmul(p_logits[:, P:3 * P], qk[a:a + MOBA_DIM, q, P:T], qk[a:a + MOBA_DIM, k, :],
                                 start=True, stop=True).then_inc(logits_made, 1)

            def moba_transposes(h):
                pe.wait_ge(probs_normed, 2 * h + 2)
                if h:
                    pe.wait_ge(moba_read, h)
                for b in range(3):
                    ins = nc.tensor.transpose(p_moba[:, b * P:(b + 1) * P], scratch[:, b * P:(b + 1) * P], ident[:, :])
                ins.then_inc(pt_made, 1)

            def moba_values(h):
                pe.wait_ge(pt_read, h + 1)
                a = (h % 2) * MOBA_DIM
                v = nat_c[:, :, h * MOBA_DIM:(h + 1) * MOBA_DIM]
                nc.tensor.matmul(p_moba[a:a + MOBA_DIM, 0:T], v[:, 0, :], probs_t[:, 0:T], start=True, stop=False)
                nc.tensor.matmul(p_moba[a:a + MOBA_DIM, P:T], v[:, 1, :], probs_t[:, T:T + P], start=False, stop=True
                                 ).then_inc(moba_made, 1)

            def ret_scores_of(j):
                if j >= 1:
                    pe.wait_ge(rs_read, 2 * j)
                nc.tensor.matmul(p_ret[:, 0:T], qk[:, 4 + j, 0:P], qk[:, j, :], start=True, stop=True)
                nc.tensor.matmul(p_ret[:, T:T + P], qk[:, 4 + j, P:T], qk[:, j, P:T], start=True, stop=True
                                 ).then_inc(rs_made, 1)

            def ret_values(j):
                pe.wait_ge(rs_read, 2 * j + 2)
                if j:
                    pe.wait_ge(rt_lo, j)
                else:
                    pe.wait_ge(cols_made, 2)
                v = nat_b[:, :, j * RET_V:(j + 1) * RET_V]
                nc.tensor.matmul(p_retv[:, 0:RET_V], ret_scores[:, 0:P], v[:, 0, :], start=True, stop=True)
                nc.tensor.matmul(p_retv[:, RET_V:], ret_scores[:, P:T], v[:, 0, :], start=True, stop=False)
                nc.tensor.matmul(p_retv[:, RET_V:], ret_scores[:, T:T + P], v[:, 1, :], start=False, stop=True
                                 ).then_inc(rv_made, 1)

            def ret_turn(j):
                pe.wait_ge(ret_done, j + 1)
                for k in range(2):
                    for t in range(2):
                        a = j * RET_V + k * P
                        ins = nc.tensor.transpose(p_retv[:, k * T + t * P:k * T + (t + 1) * P],
                                                  nat_a[:, t, a:a + P], ident[:, :])
                ins.then_inc(rt_made, 1)

            for u in range(U_NAT, U_GATE):
                n, half = divmod(u - U_NAT, 2)
                o = O_NAT + n
                if half == 0:
                    output_free(o)
                natural_unit(u, act_a, o % 2, half)
                if u == U_GATE - 2:
                    first_scores()

            for i in range(MOBA_HEADS):
                slot, rnd = unit(U_GATE + i)
                o = O_GATE + i
                output_free(o)
                unit_ready(slot, rnd)
                half_wide(slot, act_a, o % 2, 0)
                moba_transposes(i)
                if i == 0:
                    pe.wait_ge(out_read, O_GATE)
                if i % 2 == 0:
                    ret_values(i // 2)
                else:
                    ret_turn(i // 2)
                if i + 1 < MOBA_HEADS:
                    moba_scores(i + 1)
                half_wide(slot, act_a, o % 2, 1).then_inc(units_used, 1)
                if i % 2 == 1 and i + 1 < MOBA_HEADS:
                    ret_scores_of(i // 2 + 1)
                moba_values(i)

            for u in range(U_RET, U_MOBA):
                o = O_RET + u - U_RET
                output_free(o)
                wide_unit(*unit(u), act_b, o % 2, (rt_lo, 0, 2) if u == U_RET else None)

            for u in range(U_MOBA, U_OUT):
                slot = u % SLOTS
                unit_ready(*unit(u))
                for n in range(4):
                    o = O_MOBA + 2 * (u - U_MOBA) + n // 2
                    if n % 2 == 0:
                        output_free(o)
                    if u == U_MOBA and n == 0:
                        pe.wait_ge(mt_lo, 4)
                    ins = transposed(mid(w_hi, slot), mid(w_lo, slot), act_c, n * P, pair[o % 2][:, n % 2, :])
                    if n == 1:
                        ins.then_inc(half_made, 1)
                ins.then_inc(units_used, 1)

            def x2_turn(n):
                if n:
                    pe.wait_ge(xt_lo, KD + 4)
                for t in range(2):
                    pe.wait_ge(x2_made, 2 * n + t + 1)
                    for k in range(4 * n, 4 * n + 4):
                        ins = nc.tensor.transpose(x_bank(k)[:, t * P:(t + 1) * P],
                                                  nat_b[:, t, k * P:(k + 1) * P], ident[:, :])
                        if t == 1:
                            ins.then_inc(xt_made, 1)

            for u in range(U_OUT, U_MLP):
                half, n = divmod(u - U_OUT, 2)
                if half == 0:
                    output_free(O_OUT + n)
                pe.wait_ge(merged_lo, 2 * half + 2)
                natural_unit(u, act_a, (O_OUT + n) % 2, half,
                             between=(lambda: x2_turn(0)) if u == U_MLP - 1 else None)

            def up_unit(kind, c, half):
                wide_unit(kind[0], kind[1] + c, act_b, (O_UP + half) % 2)

            def down_unit(kind, c, half, first=False, final=False):
                slot = kind[0]
                unit_ready(slot, kind[1] + c)
                pe.wait_ge(hid_lo, 2 * c + 1 + half)
                hi, lo = long(w_hi, slot), long(w_lo, slot)
                def product(t, f, part, w, n, start=False, stop=False):
                    return nc.tensor.matmul(bank[2 * t + n][:, :], act_c[:, 2 * half + f, part, t * P:(t + 1) * P],
                                            w[:, f, n * 512:(n + 1) * 512], start=start, stop=stop)

                for t in range(2):
                    if final:
                        for n in range(2):
                            for f in range(2):
                                product(t, f, 0, hi, n)
                                product(t, f, 0, lo, n)
                                ins = product(t, f, 1, hi, n, stop=(f == 1))
                            ins.then_inc(down_made, 1)
                        continue
                    for f in range(2):
                        for n in range(2):
                            product(t, f, 0, hi, n, start=(first and f == 0))
                            product(t, f, 0, lo, n)
                        for n in range(2):
                            ins = product(t, f, 1, hi, n)
                if not final:
                    ins.then_inc(units_used, 1)

            for part in range(2):
                for half in range(2):
                    slot, rnd = unit(U_MLP + half)
                    if part == 0:
                        unit_ready(slot, rnd)
                        pe.wait_ge(x2_made, 2 + 2 * half)
                    for n in range(2):
                        ins = half_wide(slot, act_b, (O_UP + half) % 2, n, (xt_lo, KD, 1),
                                        range(4 * part, 4 * part + 4))
                    if part == 0 and half == 0:
                        x2_turn(1)
                    if part == 1:
                        ins.then_inc(units_used, 1)

            def mlp_round(c, first):
                down_unit(DOWN_A, c, 0, first=first)
                pe.wait_ge(out_read, O_OUT + 2 * c + 1)
                up_unit(UP_A, c, 0)
                down_unit(DOWN_B, c, 1)
                pe.wait_ge(out_read, O_OUT + 2 * c + 2)
                up_unit(UP_B, c, 1)

            mlp_round(0, True)
            with pe.Fori(1, MLP_CHUNKS - 1) as c:
                mlp_round(c, False)
            down_unit(DOWN_A, MLP_CHUNKS - 1, 0)
            down_unit((3, 9), MLP_CHUNKS - 1, 1, final=True)


def kernel(x, norm1_g, w_in, b_gate, w_ret_o, w_moba_o, w_out, norm2_g, w_up, w_down, normf_g):
    import numpy as np

    import concourse.bacc as bacc
    from concourse.bass_utils import run_bass_kernel_spmd

    given = {
        "x": x, "norm1_g": norm1_g, "w_in": w_in, "b_gate": b_gate, "w_ret_o": w_ret_o, "w_moba_o": w_moba_o,
        "w_out": w_out, "norm2_g": norm2_g, "w_up": w_up, "w_down": w_down, "normf_g": normf_g,
        "consts": constants(),
    }
    nc = bacc.Bacc("TRN2", target_bir_lowering=False, num_devices=1)
    arrays, args = {}, []
    for name, value in given.items():
        a = np.ascontiguousarray(value)
        arrays[f"{name}_dram"] = a
        args.append(nc.dram_tensor(f"{name}_dram", a.shape, mybir.dt.from_np(a.dtype), kind="ExternalInput").ap())
    args.append(nc.dram_tensor("out_dram", (1, T, D), F32, kind="ExternalOutput").ap())
    hybrid_block(nc, *args)
    r = run_bass_kernel_spmd(nc, [arrays], core_ids=[0])
    return r.results[0]["out_dram"]
```

```python
from contextlib import ExitStack

import concourse.bass as bass
from concourse import mybir

ALU = mybir.AluOpType
ACT = mybir.ActivationFunctionType
AX_X = mybir.AxisListType.X
F32 = mybir.dt.float32
F32R = mybir.dt.float32r

P = 128
T = 256
D = 1024
KD = D // P
RET_HEADS, RET_V = 4, 256
MOBA_HEADS, MOBA_DIM = 8, 64
EPS = 1e-6
RET_SCALE_COLS = RET_HEADS * T
N_CONST = P + RET_SCALE_COLS + 3 * P

SLOTS = 4
AHEAD = SLOTS - 1
UNIT = 2048
QUARTER = UNIT // 4

START_ORDER = (("w", 0), ("x", 0), ("x", 1), ("w", 1), ("x", 2), ("x", 3), ("x", 4), ("w", 2), ("x", 5),
               ("w", 3), ("x", 6), ("x", 7))

U_QK, U_NAT, U_GATE, U_RET, U_MOBA, U_OUT, U_MLP, U_END = 0, 8, 18, 26, 30, 32, 36, 68
O_QK, O_NAT, O_GATE, O_RET, O_MOBA, O_OUT, O_UP = 0, 8, 13, 21, 25, 29, 31
S_QK, S_GATE, S_RET, S_UP = 0, 8, 16, 24
MLP_CHUNKS = 8
WARM_UP, WARM_GAP = 7, 4
FIRST_UNITS = 3
U_ROUND = U_MLP + 2
UP_A, DOWN_A, UP_B, DOWN_B = [(u % SLOTS, u // SLOTS) for u in range(U_ROUND, U_ROUND + 4)]
LAST_A, LAST_B = [(u % SLOTS, u // SLOTS) for u in (U_END - 2, U_END - 1)]


def constants():
    import numpy as np

    out = np.zeros((P, N_CONST), np.float32)
    out[:, :P] = np.eye(P)
    key = np.arange(P)[:, None]
    query = np.arange(T)[None, :]
    for h in range(RET_HEADS):
        log_g = np.log1p(-np.exp2(-5.0 - h))
        diff = query - key
        decay = np.where(diff >= 0, np.exp(log_g * np.maximum(diff, 0)), 0.0) * P ** -0.5
        out[:, P + h * T:P + (h + 1) * T] = decay
    q, k = np.arange(P)[:, None], np.arange(T)[None, :]
    far = np.float32(1e32)
    out[:, -3 * P:-2 * P] = np.where(k[:, :P] <= q, q - k[:, :P], far)
    out[:, -2 * P:] = np.where(k <= q + P, q + P - k, far)
    return out


def hybrid_block(nc, x, norm1_g, w_in, b_gate, w_ret_o, w_moba_o, w_out, norm2_g, w_up, w_down,
                 normf_g, consts, out):
    x_v = x[0].rearrange("(t p) d -> p t d", p=P)
    out_v = out[0].rearrange("(t p) d -> p t d", p=P)
    w_in_v = w_in[0].rearrange("(k p) n -> p k n", p=P)
    w_ret_v = w_ret_o[0].rearrange("(k p) n -> p k n", p=P)
    w_moba_v = w_moba_o[0].rearrange("(k p) n -> p k n", p=P)
    w_out_v = w_out[0].rearrange("(k p) n -> p k n", p=P)
    w_up_v = w_up[0].rearrange("(k p) n -> p k n", p=P)
    w_down_v = w_down[0].rearrange("(k p) n -> p k n", p=P)

    with ExitStack() as ctx:
        def sb(name, shape, dt=F32):
            return ctx.enter_context(nc.sbuf_tensor(name, shape, dt))

        def sem(name):
            return ctx.enter_context(nc.semaphore(name))

        w_raw = sb("w_raw", [P, SLOTS, UNIT])
        w_hi = sb("w_hi", [P, SLOTS, UNIT], F32R)
        w_lo = sb("w_lo", [P, SLOTS, UNIT], F32R)
        act_a = sb("act_a", [P, KD, 2, T], F32R)
        act_b = sb("act_b", [P, KD, 2, T], F32R)
        act_c = sb("act_c", [P, 4, 2, T], F32R)
        qk = sb("qk", [P, 16, T])
        gates = sb("gates", [P, 16, T])
        nat_a = sb("nat_a", [P, 2, D])
        nat_b = sb("nat_b", [P, 2, D])
        nat_c = sb("nat_c", [P, 2, 512])
        side = sb("side", [P, 2, T])
        scratch = sb("scratch", [P, 3 * P])
        probs_t = sb("probs_t", [P, 3 * P])
        ret_scores = sb("ret_scores", [P, 3 * P])
        ret_junk = sb("ret_junk", [P, RET_V])
        decay = sb("decay", [P, RET_HEADS, T])
        distance = sb("distance", [P, 3 * P])
        branch = sb("branch", [P, 2, T])
        moba_out = sb("moba_out", [P, T])
        ones = sb("ones", [P, P])
        rstd_row = sb("rstd_row", [P, T])
        ident = sb("ident", [P, P])
        g1_rows = sb("g1_rows", [8, P])
        rows = sb("rows", [24, P])
        cols = sb("cols", [P, 32])
        sq = sb("sq", [P, 8])
        ms = sb("ms", [P, 8])
        rstd = sb("rstd", [P, 8])
        neg_half = sb("neg_half", [P, 2])
        top = sb("top", [P, 4])
        neg_top = sb("neg_top", [P, 2])
        prob_sum = sb("prob_sum", [P, 2])
        prob_inv = sb("prob_inv", [P, 2])

        up_sum = qk[:, 0:2, :]
        up_sqr = qk[:, 2:4, :]
        merged = qk[:, 8:12, :].rearrange("p (m k) t -> p m k t", m=2)
        diag = scratch[:, 0:T]
        junk = qk[:, 8:12, :].rearrange("p a b -> p (a b)")
        gf = nat_c[:, :, :].rearrange("p a b -> p (a b)")

        pair = [ctx.enter_context(nc.psum_tensor(f"pair{i}", [P, 2, 512], F32)) for i in range(2)]
        bank = [ctx.enter_context(nc.psum_tensor(f"bank{i}", [P, 512], F32)) for i in range(4, 8)]
        p_logits, p_moba, p_ret, p_retv = bank

        x_loaded = [sem(f"x_loaded{n}") for n in range(2)]
        first_half = [sem(f"first_half{u}") for u in range(2)]
        ones_made = sem("ones_made")
        g1_loaded = sem("g1_loaded")
        ident_loaded = sem("ident_loaded")
        rows_loaded = sem("rows_loaded")
        consts_loaded = sem("consts_loaded")
        x_again = sem("x_again")
        gf_loaded = sem("gf_loaded")
        w_loaded = [sem(f"w_loaded{i}") for i in range(SLOTS)]
        hi_made = sem("hi_made")
        lo_made = sem("lo_made")
        first_hi = sem("first_hi")
        first_lo = sem("first_lo")
        units_used = sem("units_used")
        half_made = sem("half_made")
        out_read = sem("out_read")
        side_made = sem("side_made")
        const_half = sem("const_half")
        sq_made = sem("sq_made")
        ms_made = sem("ms_made")
        rstd_made = sem("rstd_made")
        diag_made = sem("diag_made")
        row_t = sem("row_t")
        row_made = sem("row_made")
        cols_t = sem("cols_t")
        cols_made = sem("cols_made")
        xt_made = sem("xt_made")
        xt_hi = sem("xt_hi")
        xt_lo = sem("xt_lo")
        scaled_made = sem("scaled_made")
        rg_sig = sem("rg_sig")
        dve_step = sem("dve_step")
        logits_made = sem("logits_made")
        logits_read = sem("logits_read")
        top_made = sem("top_made")
        probs_made = sem("probs_made")
        probs_normed = sem("probs_normed")
        pt_made = sem("pt_made")
        pt_read = sem("pt_read")
        moba_made = sem("moba_made")
        moba_read = sem("moba_read")
        mt_hi = sem("mt_hi")
        mt_lo = sem("mt_lo")
        rs_made = sem("rs_made")
        rs_read = sem("rs_read")
        rv_made = sem("rv_made")
        ret_sq = sem("ret_sq")
        ret_ms = sem("ret_ms")
        ret_rstd = sem("ret_rstd")
        ret_done = sem("ret_done")
        rt_made = sem("rt_made")
        rt_hi = sem("rt_hi")
        rt_lo = sem("rt_lo")
        gate_sig = sem("gate_sig")
        gated_made = sem("gated_made")
        merged_made = sem("merged_made")
        merged_hi = sem("merged_hi")
        merged_lo = sem("merged_lo")
        x2_made = sem("x2_made")
        x2_sq = sem("x2_sq")
        hid_made = sem("hid_made")
        hid_hi = sem("hid_hi")
        hid_lo = sem("hid_lo")
        down_made = sem("down_made")
        x3_made = sem("x3_made")
        x3_sq = sem("x3_sq")
        x3_ms = sem("x3_ms")
        x3_rstd = sem("x3_rstd")
        x3_gained = sem("x3_gained")
        y_first = sem("y_first")
        y_second = sem("y_second")
        y_stored = sem("y_stored")

        def unit_source(u):
            if u < U_NAT:
                c = 256 * u + (2048 if u >= 4 else 0)
                return w_in_v[:, :, c:c + 256]
            if u < U_GATE:
                n, half = divmod(u - U_NAT, 2)
                c = [2048, 2560, 1024, 1536, 4096][n]
                return w_in_v[:, 4 * half:4 * half + 4, c:c + 512]
            if u < U_RET:
                c = 4608 + 256 * (u - U_GATE)
                return w_in_v[:, :, c:c + 256]
            if u < U_MOBA:
                c = 256 * (u - U_RET)
                return w_ret_v[:, :, c:c + 256]
            if u < U_OUT:
                c = 512 * (u - U_MOBA)
                return w_moba_v[:, :, c:c + 512]
            half, n = divmod(u - U_OUT, 2)
            return w_out_v[:, 4 * half:4 * half + 4, 512 * n:512 * n + 512]

        def unit(u):
            return u % SLOTS, u // SLOTS

        def part_count(u, q):
            return u + 1 if q == 3 else 3 * u + q + 1

        def quarter(q):
            return slice(q * QUARTER, (q + 1) * QUARTER)

        def prepared(u):
            return [u + AHEAD - 1] if u < 5 else [u + AHEAD - 1, u + AHEAD] if u == 5 else [u + AHEAD]

        def output_wait(eng, o):
            if o < O_NAT:
                eng.wait_ge(units_used, o + 1)
            elif o < O_GATE:
                eng.wait_ge(units_used, U_NAT + 2 * (o - O_NAT) + 2)
            elif o < O_MOBA:
                eng.wait_ge(units_used, U_GATE + o - O_GATE + 1)
            elif o < O_OUT and (o - O_MOBA) % 2 == 0:
                eng.wait_ge(half_made, (o - O_MOBA) // 2 + 1)
            elif o < O_OUT:
                eng.wait_ge(units_used, U_MOBA + (o - O_MOBA) // 2 + 1)
            else:
                eng.wait_ge(units_used, U_OUT + 3 + o - O_OUT)

        def x_bank(k):
            return bank[k % 4][:, (k // 4) * T:(k // 4) * T + T]

        def x_first(k):
            if k < 4:
                return bank[k][:, 0:T]
            return pair[1][:, k % 2, (k - 4) // 2 * T:(k - 4) // 2 * T + T]

        def wide(ring, slot):
            return ring[:, slot, :].rearrange("p (k n) -> p k n", k=8)

        def mid(ring, slot):
            return ring[:, slot, :].rearrange("p (k n) -> p k n", k=4)

        def long(ring, slot):
            return ring[:, slot, :].rearrange("p (k n) -> p k n", k=2)

        block = ctx.enter_context(nc.Block())

        @block.sync
        def _(sp):
            def load(slot, rnd, view, source):
                if type(rnd) is not int or rnd > 0:
                    sp.wait_ge(lo_made, SLOTS * (rnd - 1) + slot + 1)
                sp.dma_start(view(w_raw, slot), source).then_inc(w_loaded[slot], 16)

            def load_before_mlp(u):
                view = mid if U_NAT <= u < U_GATE or u >= U_MOBA else wide
                load(u % SLOTS, u // SLOTS, view, unit_source(u))

            def load_up(kind, c, half):
                load(kind[0], kind[1] + c, wide, w_up_v[:, :, bass.ds(512 * (c + 1) + 256 * half, 256)])

            def load_down(kind, c, half):
                load(kind[0], kind[1] + c, long, w_down_v[:, bass.ds(4 * c + 2 * half, 2), :])

            for u in range(2):
                for n in range(2):
                    if u == 0:
                        part = slice(512 * n, 512 * n + 512)
                        sp.dma_start(nat_b[:, :, part], x_v[:, :, part]).then_inc(x_loaded[n], 16)
                    sp.dma_start(wide(w_raw, u)[:, 4 * n:4 * n + 4, :], unit_source(u)[:, 4 * n:4 * n + 4, :]
                                 ).then_inc(w_loaded[u] if n else first_half[u], 16)
            for u in range(2, SLOTS):
                load_before_mlp(u)
            sp.dma_start(rows[0:8, :], norm2_g.rearrange("a (k p) -> (a k) p", p=P)).then_inc(rows_loaded, 16)
            sp.dma_start(rows[8:24, :], b_gate.rearrange("a (k p) -> (a k) p", p=P)).then_inc(rows_loaded, 16)
            sp.dma_start(decay[:, :, :], consts[:, P:P + RET_SCALE_COLS].rearrange("p (h t) -> p h t", h=RET_HEADS)
                         ).then_inc(consts_loaded, 16)
            sp.dma_start(distance[:, :], consts[:, P + RET_SCALE_COLS:]).then_inc(consts_loaded, 16)
            for u in range(SLOTS, U_OUT):
                load_before_mlp(u)
            sp.wait_ge(rv_made, RET_HEADS)
            sp.dma_start(nat_b[:, :, :], x_v).then_inc(x_again, 16)
            sp.wait_ge(moba_made, MOBA_HEADS)
            sp.dma_start(gf, normf_g.rearrange("(a d) -> a d", a=1).to_broadcast([P, D])).then_inc(gf_loaded, 16)
            for u in range(U_OUT, U_MLP):
                load_before_mlp(u)
            for half in range(2):
                load(*unit(U_MLP + half), wide, w_up_v[:, :, 256 * half:256 * half + 256])
            with sp.Fori(0, MLP_CHUNKS - 1) as c:
                load_up(UP_A, c, 0)
                load_down(DOWN_A, c, 0)
                load_up(UP_B, c, 1)
                load_down(DOWN_B, c, 1)
            load(*LAST_A, long, w_down_v[:, 28:30, :])
            load(*LAST_B, long, w_down_v[:, 30:32, :])
            for t in range(2):
                for n, made in enumerate((y_first, y_second)):
                    sp.wait_ge(made, t + 1)
                    sp.dma_start(out_v[:, t, 512 * n:512 * n + 512], nat_b[:, t, 512 * n:512 * n + 512]
                                 ).then_inc(y_stored, 16)
            sp.wait_ge(y_stored, 64)

        @block.gpsimd
        def _(pool):
            nc.gpsimd.memset(neg_half[:, :], -0.5).then_inc(const_half, 1)
            pool.wait_ge(const_half, 1)

            def power(wanted, count, source, made, width):
                pool.wait_ge(wanted, count)
                nc.gpsimd.tensor_tensor(rstd[:, source:source + width], ms[:, source:source + width],
                                        neg_half[:, 0:width], ALU.pow).then_inc(made, 1)

            power(ms_made, 1, 0, rstd_made, 2)

            factors = rstd_row[:, :].rearrange("p (a t) -> p a t", a=1).to_broadcast([P, 2, T])

            def scaled(o, into):
                pool.wait_ge(out_read, o + 1)
                nc.gpsimd.tensor_tensor(into, branch[:, :, :], factors, ALU.mult).then_inc(scaled_made, 1)

            pool.wait_ge(row_made, 1)
            for n in range(8):
                scaled(O_QK + n, qk[:, 2 * n:2 * n + 2, :])
            for i in range(MOBA_HEADS):
                if i:
                    scaled(O_GATE + i - 1, gates[:, 2 * i - 2:2 * i, :])
                if i % 2 == 0:
                    if i:
                        pool.wait_ge(ret_done, i // 2)
                    power(ret_ms, i // 2 + 1, 2, ret_rstd, 2)
            scaled(O_RET - 1, gates[:, 14:16, :])
            for m in range(4):
                pool.wait_ge(gated_made, 4 + m + 1)
                if m >= 2:
                    pool.wait_ge(merged_lo, m - 1)
                nc.gpsimd.tensor_tensor(merged[:, m % 2, :, :], gates[:, 2 * m:2 * m + 2, :],
                                        gates[:, 8 + 2 * m:10 + 2 * m, :], ALU.add).then_inc(merged_made, 1)
            for t in range(2):
                power(x3_ms, t + 1, 6 + t, x3_rstd, 1)

        @block.scalar
        def _(act):
            def make_hi(slot, rnd):
                act.wait_ge(w_loaded[slot], 16 * rnd + 16)
                if type(rnd) is not int or rnd > 0:
                    act.wait_ge(units_used, SLOTS * (rnd - 1) + slot + 1)
                nc.scalar.copy(w_hi[:, slot, :], w_raw[:, slot, :]).then_inc(hi_made, 1)

            def make_side(o):
                output_wait(act, o)
                if o > 0:
                    act.wait_ge(out_read, o)
                nc.scalar.copy(side[:, :, :], pair[o % 2][:, :, T:]).then_inc(side_made, 1)

            act.dma_start(ident[:, :], consts[:, 0:P]).then_inc(ident_loaded, 16)
            act.dma_start(g1_rows[:, :], norm1_g.rearrange("a (k p) -> (a k) p", p=P)).then_inc(g1_loaded, 16)

            def x_squares(n):
                act.wait_ge(x_loaded[n], 16)
                for t in range(2):
                    if n or t:
                        act.wait_ge(sq_made, 2 * n + t)
                    nc.scalar.activation(junk[:, 0:512], nat_b[:, t, 512 * n:512 * n + 512], ACT.Square,
                                         accum_out=sq[:, 2 * n + t:2 * n + t + 1]).then_inc(sq_made, 1)

            def hi_quarter(u, q):
                if q == 0 and u < 2:
                    act.wait_ge(first_half[u], 16)
                elif q == 2 or q == 0:
                    act.wait_ge(w_loaded[u], 16)
                nc.scalar.copy(w_hi[:, u, quarter(q)], w_raw[:, u, quarter(q)]
                               ).then_inc(hi_made if q == 3 else first_hi, 1)

            x_squares(0)
            for kind, k in START_ORDER:
                if kind == "w":
                    hi_quarter(0, k)
                    continue
                if k == 0:
                    act.wait_ge(cols_made, 1)
                act.wait_ge(xt_made, k + 1 if k < 4 else KD)
                if k >= 6:
                    act.wait_ge(xt_lo, k - 1)
                nc.scalar.activation(act_a[:, k, 0, :], x_first(k), ACT.Copy,
                                     scale=cols[:, k:k + 1]).then_inc(xt_hi, 1)
            for q in range(4):
                hi_quarter(1, q)
            make_side(O_QK)
            x_squares(1)
            for q in range(4):
                hi_quarter(2, q)

            for u in range(U_QK + 1, U_NAT):
                if u > 1:
                    make_side(O_QK + u - 1)
                for v in prepared(u):
                    make_hi(*unit(v))
            for u in range(U_NAT, U_GATE):
                if u == U_NAT:
                    make_side(O_NAT - 1)
                if u in (U_NAT + 2, U_NAT + 4):
                    n = (u - U_NAT) // 2 - 1
                    output_wait(act, O_NAT + n)
                    for t in range(2):
                        nc.scalar.activation(nat_a[:, t, 512 * n:512 * n + 512], pair[(O_NAT + n) % 2][:, t, :],
                                             ACT.Sigmoid, scale=rstd[:, t:t + 1]).then_inc(rg_sig, 1)
                make_hi(*unit(u + AHEAD))

            def softmax(h):
                act.wait_ge(top_made, h + 1)
                if h:
                    act.wait_ge(probs_normed, 2 * h)
                for t, (a, b) in enumerate(((0, P), (P, 3 * P))):
                    nc.scalar.activation(scratch[:, a:b], scratch[:, a:b], ACT.Exp, bias=neg_top[:, t:t + 1],
                                         scale=MOBA_DIM ** -0.5, accum_out=prob_sum[:, t:t + 1]
                                         ).then_inc(probs_made, 1)

            def probs_out(h):
                act.wait_ge(pt_made, h + 1)
                if h:
                    act.wait_ge(moba_made, h)
                nc.scalar.copy(probs_t[:, :], p_moba[:, 0:3 * P]).then_inc(pt_read, 1)

            def ret_squares(j):
                act.wait_ge(rv_made, j + 1)
                if j:
                    act.wait_ge(ret_ms, j)
                for t in range(2):
                    if j or t:
                        act.wait_ge(ret_sq, 2 * j + t)
                    nc.scalar.activation(ret_junk[:, :], p_retv[:, t * RET_V:(t + 1) * RET_V], ACT.Square,
                                         accum_out=sq[:, 2 + t:3 + t]).then_inc(ret_sq, 1)

            def ret_hi(j):
                act.wait_ge(rt_made, j + 1)
                nc.scalar.copy(act_b[:, 2 * j:2 * j + 2, 0, :], p_retv[:, :].rearrange("p (k t) -> p k t", k=2)
                               ).then_inc(rt_hi, 1)

            def moba_copy(h):
                a = (h % 2) * MOBA_DIM
                act.wait_ge(moba_made, h + 1)
                if h >= 2 and h % 2 == 0:
                    act.wait_ge(mt_lo, h // 2)
                nc.scalar.copy(moba_out[a:a + MOBA_DIM, :], p_moba[a:a + MOBA_DIM, 0:T]).then_inc(moba_read, 1)

            def moba_hi(p):
                act.wait_ge(moba_read, 2 * p + 2)
                nc.scalar.copy(act_c[:, p, 0, :], moba_out[:, :]).then_inc(mt_hi, 1)

            def sigmoids(first):
                act.wait_ge(cols_made, 2)
                for g in range(first, first + 8):
                    nc.scalar.activation(gates[:, g, :], gates[:, g, :], ACT.Sigmoid,
                                         bias=cols[:, 16 + g:17 + g]).then_inc(gate_sig, 1)

            softmax(0)
            for i in range(MOBA_HEADS):
                u = U_GATE + i
                if i > 0:
                    moba_copy(i - 1)
                    make_side(O_GATE + i - 1)
                    if i % 2 == 0:
                        moba_hi(i // 2 - 1)
                probs_out(i)
                if i == MOBA_HEADS - 1:
                    ret_hi(i // 2)
                make_hi(*unit(u + AHEAD))
                if i + 1 < MOBA_HEADS:
                    softmax(i + 1)
                    if i % 2 == 0:
                        ret_squares(i // 2)
                    else:
                        ret_hi(i // 2)
            for u in range(U_RET, U_MOBA):
                make_side(O_RET - 1 + u - U_RET)
                make_hi(*unit(u + AHEAD))
                if u == U_RET:
                    sigmoids(0)
                    moba_copy(MOBA_HEADS - 1)
                    moba_hi(3)
                elif u == U_RET + 1:
                    act.wait_ge(scaled_made, S_RET)
                    sigmoids(8)

            def merged_out(m):
                act.wait_ge(merged_made, m + 1)
                nc.scalar.copy(act_a[:, 2 * m:2 * m + 2, 0, :], merged[:, m % 2, :, :]).then_inc(merged_hi, 1)

            make_side(O_RET + 3)
            make_hi(*unit(U_MOBA + AHEAD))
            make_side(O_MOBA)
            for m in range(4):
                if m < 3:
                    make_side(O_MOBA + m + 1)
                merged_out(m)

            def x2_squares(n):
                for t in range(2):
                    act.wait_ge(x2_made, 2 * n + t + 1)
                    if n or t:
                        act.wait_ge(x2_sq, 2 * n + t)
                    nc.scalar.activation(junk[:, 0:512], nat_b[:, t, 512 * n:512 * n + 512], ACT.Square,
                                         accum_out=sq[:, 4 + 2 * n + t:5 + 2 * n + t]).then_inc(x2_sq, 1)

            def x2_hi(n):
                for k in range(4 * n, 4 * n + 4):
                    act.wait_ge(xt_made, KD + k + 1)
                    nc.scalar.activation(act_b[:, k, 0, :], x_bank(k), ACT.Copy,
                                         scale=cols[:, 8 + k:9 + k]).then_inc(xt_hi, 1)

            for u in range(U_OUT - 1, U_OUT + 3):
                make_hi(*unit(u + AHEAD))
            x2_hi(0)
            x2_hi(1)
            make_hi(*unit(U_OUT + 3 + AHEAD))

            def hidden_out(n, half):
                act.wait_ge(hid_made, n + 1)
                nc.scalar.copy(act_c[:, 2 * half:2 * half + 2, 0, :], up_sqr).then_inc(hid_hi, 1)

            def up_side(used, n, half):
                act.wait_ge(units_used, used)
                act.wait_ge(out_read, O_OUT + n)
                nc.scalar.copy(side[:, :, :], pair[(O_UP + half) % 2][:, :, T:]).then_inc(side_made, 1)

            for half in range(2):
                up_side(U_MLP + half + 1, half, half)
                make_hi(*unit(U_MLP + half + AHEAD))
                hidden_out(half, half)
            make_hi(*unit(U_MLP + 2 + AHEAD))

            def mlp_slots(c, last):
                up_side(U_ROUND + 1 + 4 * c, 2 * c + 2, 0)
                make_hi(UP_A[0], UP_A[1] + 1 + c)
                act.wait_ge(units_used, U_ROUND + 2 + 4 * c)
                hidden_out(2 * c + 2, 0)
                make_hi(DOWN_A[0], DOWN_A[1] + 1 + c)
                up_side(U_ROUND + 3 + 4 * c, 2 * c + 3, 1)
                if last:
                    x2_squares(0)
                    x2_squares(1)
                else:
                    make_hi(UP_B[0], UP_B[1] + 1 + c)
                act.wait_ge(units_used, U_ROUND + 4 + 4 * c)
                hidden_out(2 * c + 3, 1)
                if not last:
                    make_hi(DOWN_B[0], DOWN_B[1] + 1 + c)

            with act.Fori(0, MLP_CHUNKS - 2) as c:
                mlp_slots(c, False)
            mlp_slots(MLP_CHUNKS - 2, True)

            def y(t):
                act.wait_ge(x3_rstd, t + 1)
                act.wait_ge(x3_gained, t + 1)
                nc.scalar.activation(nat_b[:, t, 0:512], nat_b[:, t, 0:512], ACT.Copy, scale=rstd[:, 6 + t:7 + t]
                                     ).then_inc(y_first, 1)

            for t in range(2):
                if t == 1:
                    y(0)
                for n in range(2):
                    act.wait_ge(x3_made, 2 * t + n + 1)
                    if t or n:
                        act.wait_ge(x3_sq, 2 * t + n)
                    nc.scalar.activation(junk[:, 0:512], nat_a[:, t, 512 * n:512 * n + 512], ACT.Square,
                                         accum_out=sq[:, 2 * t + n:2 * t + n + 1]).then_inc(x3_sq, 1)
            y(1)

        @block.vector
        def _(dve):
            steps = [0]

            def link(ins):
                steps[0] += 1
                ins.then_inc(dve_step, 1)
                dve.wait_ge(dve_step, steps[0])

            def make_lo(slot, rnd):
                dve.wait_ge(hi_made, SLOTS * rnd + slot + 1)
                nc.vector.tensor_tensor(w_lo[:, slot, :], w_raw[:, slot, :], w_hi[:, slot, :].bitcast(F32),
                                        ALU.subtract).then_inc(lo_made, 1)

            def add_side(o, s, parity, into):
                dve.wait_ge(side_made, s + 1)
                nc.vector.tensor_tensor(into, pair[parity][:, :, 0:T], side[:, :, :], ALU.add).then_inc(out_read, 1)

            nc.vector.memset(ones[:, :], 1.0).then_inc(ones_made, 1)

            def branch_out(o, s):
                if s:
                    dve.wait_ge(scaled_made, s)
                add_side(o, s, o % 2, branch[:, :, :])

            def lo_quarter(u, q):
                dve.wait_ge(hi_made if q == 3 else first_hi, part_count(u, q))
                nc.vector.tensor_tensor(w_lo[:, u, quarter(q)], w_raw[:, u, quarter(q)],
                                        w_hi[:, u, quarter(q)].bitcast(F32), ALU.subtract
                                        ).then_inc(lo_made if q == 3 else first_lo, 1)

            dve.wait_ge(cols_t, 1)
            nc.vector.tensor_copy(cols[:, 0:8], pair[0][:, 1, 0:8]).then_inc(cols_made, 1)
            dve.wait_ge(cols_made, 1)
            for kind, k in START_ORDER:
                if kind == "w":
                    lo_quarter(0, k)
                    continue
                dve.wait_ge(xt_hi, k + 1)
                nc.vector.scalar_tensor_tensor(out=act_a[:, k, 1, :], in0=x_first(k),
                                               scalar=cols[:, k:k + 1], in1=act_a[:, k, 0, :].bitcast(F32),
                                               op0=ALU.mult, op1=ALU.subtract).then_inc(xt_lo, 1)
            for q in range(4):
                lo_quarter(1, q)
            branch_out(O_QK, S_QK)
            dve.wait_ge(sq_made, 4)
            link(nc.vector.tensor_tensor(ms[:, 0:2], sq[:, 0:2], sq[:, 2:4], ALU.add))
            nc.vector.tensor_scalar(ms[:, 0:2], ms[:, 0:2], 1.0 / D, EPS, ALU.mult, ALU.add).then_inc(ms_made, 1)
            dve.wait_ge(ident_loaded, 16)
            for q in range(4):
                if q == 1:
                    dve.wait_ge(rstd_made, 1)
                    for t in range(2):
                        nc.vector.tensor_scalar(diag[:, t * P:(t + 1) * P], ident[:, :], rstd[:, t:t + 1], None,
                                                ALU.mult).then_inc(diag_made, 1)
                lo_quarter(2, q)
            dve.wait_ge(row_t, 1)
            nc.vector.tensor_copy(rstd_row[:, :], p_logits[:, 0:T]).then_inc(row_made, 1)
            for u in range(U_QK + 1, U_NAT):
                if u > 1:
                    branch_out(O_QK + u - 1, S_QK + u - 1)
                for v in prepared(u):
                    make_lo(*unit(v))

            def natural_out(n):
                o = O_NAT + n
                if n < 2:
                    dve.wait_ge(rg_sig, 2 * n + 2)
                else:
                    output_wait(dve, o)
                for t in range(2):
                    source = pair[o % 2][:, t, :]
                    if n < 2:
                        part = nat_a[:, t, 512 * n:512 * n + 512]
                        ins = nc.vector.scalar_tensor_tensor(out=part, in0=source, scalar=rstd[:, t:t + 1], in1=part,
                                                             op0=ALU.mult, op1=ALU.mult)
                    else:
                        part = nat_b[:, t, 512 * (n - 2):512 * (n - 2) + 512] if n < 4 else nat_c[:, t, :]
                        ins = nc.vector.tensor_scalar(part, source, rstd[:, t:t + 1], None, ALU.mult)
                    if t == 0:
                        link(ins)
                    else:
                        ins.then_inc(out_read, 1)

            for u in range(U_NAT, U_GATE):
                if u == U_NAT:
                    branch_out(O_NAT - 1, S_GATE - 1)
                elif (u - U_NAT) % 2 == 0:
                    natural_out((u - U_NAT) // 2 - 1)
                make_lo(*unit(u + AHEAD))

            def logits(h):
                dve.wait_ge(logits_made, h + 1)
                if h == 0:
                    dve.wait_ge(consts_loaded, 32)
                else:
                    dve.wait_ge(pt_made, h)
                slope = 2.0 ** -(h + 1)
                nc.vector.scalar_tensor_tensor(out=scratch[:, :], in0=distance[:, :], scalar=-slope * MOBA_DIM ** 0.5,
                                               in1=p_logits[:, 0:3 * P], op0=ALU.mult, op1=ALU.add
                                               ).then_inc(logits_read, 1)
                dve.wait_ge(logits_read, h + 1)
                nc.vector.reduce_max(top[:, 0:1], scratch[:, 0:P], AX_X).then_inc(dve_step, 1)
                steps[0] += 1
                link(nc.vector.reduce_max(top[:, 1:2], scratch[:, P:3 * P], AX_X))
                nc.vector.tensor_scalar(neg_top[:, :], top[:, 0:2], -MOBA_DIM ** -0.5, None, ALU.mult
                                        ).then_inc(top_made, 1)

            def decayed(j):
                dve.wait_ge(rs_made, j + 1)
                if j:
                    dve.wait_ge(rv_made, j)
                for a, b in ((0, T), (T, T + P)):
                    nc.vector.tensor_tensor(ret_scores[:, a:b], p_ret[:, a:b], decay[:, j, 0:b - a], ALU.mult
                                            ).then_inc(rs_read, 1)

            def probs_norm(h):
                dve.wait_ge(probs_made, 2 * h + 2)
                link(nc.vector.reciprocal(prob_inv[:, :], prob_sum[:, :]))
                for t, (a, b) in enumerate(((0, P), (P, 3 * P))):
                    nc.vector.tensor_scalar(scratch[:, a:b], scratch[:, a:b], prob_inv[:, t:t + 1], None, ALU.mult
                                            ).then_inc(probs_normed, 1)

            def ret_mean(j):
                dve.wait_ge(ret_sq, 2 * j + 2)
                nc.vector.tensor_scalar(ms[:, 2:4], sq[:, 2:4], 1.0 / RET_V, EPS, ALU.mult, ALU.add
                                        ).then_inc(ret_ms, 1)

            def ret_norm(j):
                dve.wait_ge(ret_rstd, j + 1)
                for t in range(2):
                    part = nat_a[:, t, j * RET_V:(j + 1) * RET_V]
                    ins = nc.vector.scalar_tensor_tensor(out=part, in0=p_retv[:, t * RET_V:(t + 1) * RET_V],
                                                         scalar=rstd[:, 2 + t:3 + t], in1=part,
                                                         op0=ALU.mult, op1=ALU.mult)
                    if t == 0:
                        link(ins)
                    else:
                        ins.then_inc(ret_done, 1)

            def ret_lo(j):
                dve.wait_ge(rt_hi, j + 1)
                nc.vector.tensor_tensor(act_b[:, 2 * j:2 * j + 2, 1, :],
                                        p_retv[:, :].rearrange("p (k t) -> p k t", k=2),
                                        act_b[:, 2 * j:2 * j + 2, 0, :].bitcast(F32), ALU.subtract).then_inc(rt_lo, 1)

            def moba_lo(p):
                dve.wait_ge(mt_hi, p + 1)
                nc.vector.tensor_tensor(act_c[:, p, 1, :], moba_out[:, :], act_c[:, p, 0, :].bitcast(F32),
                                        ALU.subtract).then_inc(mt_lo, 1)

            dve.wait_ge(cols_t, 2)
            nc.vector.tensor_copy(cols[:, 8:32], p_retv[:, 0:24]).then_inc(cols_made, 1)
            logits(0)
            decayed(0)
            natural_out(4)
            probs_norm(0)
            for i in range(MOBA_HEADS):
                u = U_GATE + i
                if i > 0:
                    o = O_GATE + i - 1
                    branch_out(o, S_GATE + i - 1)
                    if i % 2 == 0:
                        decayed(i // 2)
                        moba_lo(i // 2 - 1)
                if i + 1 < MOBA_HEADS:
                    logits(i + 1)
                if i == MOBA_HEADS - 1:
                    ret_lo(i // 2)
                make_lo(*unit(u + AHEAD))
                if i % 2 == 0:
                    ret_mean(i // 2)
                if i + 1 < MOBA_HEADS:
                    probs_norm(i + 1)
                    if i % 2 == 0:
                        ret_norm(i // 2)
                    else:
                        ret_lo(i // 2)

            gated_count = [0]

            def gated(o, pair_of_tiles, first_gate, between=None):
                if o == O_RET:
                    dve.wait_ge(scaled_made, S_RET)
                n = pair_of_tiles
                add_side(o, S_RET + o - O_RET, o % 2, branch[:, :, :])
                dve.wait_ge(out_read, o + 1)
                if between:
                    between()
                g = gates[:, first_gate + 2 * n:first_gate + 2 * n + 2, :]
                dve.wait_ge(gate_sig, first_gate + 2 * n + 2)
                nc.vector.tensor_tensor(g, branch[:, :, :], g, ALU.mult).then_inc(gated_made, 1)
                gated_count[0] += 1
                dve.wait_ge(gated_made, gated_count[0])

            for u in range(U_RET, U_MOBA):
                if u == U_RET:
                    o = O_RET - 1
                    branch_out(o, S_RET - 1)
                else:
                    gated(u - 1 - U_RET + O_RET, u - 1 - U_RET, 0)
                make_lo(*unit(u + AHEAD))
                if u == U_RET:
                    moba_lo(3)

            def merged_lo_of(m):
                dve.wait_ge(merged_hi, m + 1)
                nc.vector.tensor_tensor(act_a[:, 2 * m:2 * m + 2, 1, :], merged[:, m % 2, :, :],
                                        act_a[:, 2 * m:2 * m + 2, 0, :].bitcast(F32), ALU.subtract
                                        ).then_inc(merged_lo, 1)

            gated(O_RET + 3, 3, 0)
            gated(O_MOBA, 0, 8)
            gated(O_MOBA + 1, 1, 8)
            merged_lo_of(0)
            gated(O_MOBA + 2, 2, 8, between=lambda: merged_lo_of(1))
            make_lo(*unit(U_MOBA + AHEAD))
            gated(O_MOBA + 3, 3, 8)
            merged_lo_of(2)
            merged_lo_of(3)

            def residual(n):
                o = O_OUT + n
                if n == 0:
                    dve.wait_ge(x_again, 16)
                output_wait(dve, o)
                for t in range(2):
                    part = nat_b[:, t, 512 * n:512 * n + 512]
                    nc.vector.tensor_tensor(part, pair[o % 2][:, t, :], part, ALU.add).then_inc(x2_made, 1)

            def x2_lo(n):
                for k in range(4 * n, 4 * n + 4):
                    dve.wait_ge(xt_hi, KD + k + 1)
                    nc.vector.scalar_tensor_tensor(out=act_b[:, k, 1, :],
                                                   in0=x_bank(k),
                                                   scalar=cols[:, 8 + k:9 + k], in1=act_b[:, k, 0, :].bitcast(F32),
                                                   op0=ALU.mult, op1=ALU.subtract).then_inc(xt_lo, 1)

            for u in range(U_OUT - 1, U_OUT + 3):
                make_lo(*unit(u + AHEAD))
                if u == U_OUT + 1:
                    residual(0)
            x2_lo(0)
            residual(1)
            x2_lo(1)
            make_lo(*unit(U_OUT + 3 + AHEAD))

            def hidden_sum(n, half):
                add_side(None, S_UP + n, (O_UP + half) % 2, up_sum)
                dve.wait_ge(out_read, O_OUT + n + 1)
                nc.vector.scalar_tensor_tensor(out=up_sqr, in0=up_sum, scalar=0.0, in1=up_sum,
                                               op0=ALU.max, op1=ALU.mult).then_inc(hid_made, 1)

            def hidden_lo(n, half):
                dve.wait_ge(hid_hi, n + 1)
                nc.vector.tensor_tensor(act_c[:, 2 * half:2 * half + 2, 1, :], up_sqr,
                                        act_c[:, 2 * half:2 * half + 2, 0, :].bitcast(F32), ALU.subtract
                                        ).then_inc(hid_lo, 1)

            for half in range(2):
                if half:
                    dve.wait_ge(hid_lo, 1)
                hidden_sum(half, half)
                make_lo(*unit(U_MLP + half + AHEAD))
                hidden_lo(half, half)
            make_lo(*unit(U_MLP + 2 + AHEAD))

            def mlp_slots(c, last):
                dve.wait_ge(hid_lo, 2 * c + 2)
                hidden_sum(2 * c + 2, 0)
                make_lo(UP_A[0], UP_A[1] + 1 + c)
                hidden_lo(2 * c + 2, 0)
                make_lo(DOWN_A[0], DOWN_A[1] + 1 + c)
                dve.wait_ge(hid_lo, 2 * c + 3)
                hidden_sum(2 * c + 3, 1)
                if not last:
                    make_lo(UP_B[0], UP_B[1] + 1 + c)
                hidden_lo(2 * c + 3, 1)
                if not last:
                    make_lo(DOWN_B[0], DOWN_B[1] + 1 + c)

            with dve.Fori(0, MLP_CHUNKS - 2) as c:
                mlp_slots(c, False)
            mlp_slots(MLP_CHUNKS - 2, True)
            dve.wait_ge(x2_sq, 4)
            link(nc.vector.tensor_tensor(ms[:, 4:6], sq[:, 4:6], sq[:, 6:8], ALU.add))
            link(nc.vector.tensor_scalar(ms[:, 4:6], ms[:, 4:6], 1.0 / D, EPS, ALU.mult, ALU.add))
            link(nc.vector.reciprocal(rstd[:, 4:6], ms[:, 4:6]))

            def x3(t, n):
                dve.wait_ge(down_made, 2 * t + n + 1)
                part = slice(512 * n, 512 * n + 512)
                nc.vector.scalar_tensor_tensor(out=nat_a[:, t, part], in0=bank[2 * t + n][:, :],
                                               scalar=rstd[:, 4 + t:5 + t], in1=nat_b[:, t, part],
                                               op0=ALU.mult, op1=ALU.add).then_inc(x3_made, 1)

            def gained(t):
                dve.wait_ge(x3_made, 2 * t + 1)
                nc.vector.tensor_tensor(nat_b[:, t, 0:512], nat_a[:, t, 0:512], gf[:, 0:512], ALU.mult
                                        ).then_inc(x3_gained, 1)

            def y(t):
                dve.wait_ge(x3_rstd, t + 1)
                nc.vector.scalar_tensor_tensor(out=nat_b[:, t, 512:D], in0=nat_a[:, t, 512:D],
                                               scalar=rstd[:, 6 + t:7 + t],
                                               in1=gf[:, 512:D], op0=ALU.mult, op1=ALU.mult).then_inc(y_second, 1)

            def mean(t, n):
                dve.wait_ge(x3_sq, 2 * t + n + 1)
                mean_of_t = ms[:, 6 + t:7 + t]
                if n == 0:
                    link(nc.vector.tensor_scalar(mean_of_t, sq[:, 2 * t:2 * t + 1], 1.0 / D, EPS, ALU.mult, ALU.add))
                else:
                    nc.vector.scalar_tensor_tensor(out=mean_of_t, in0=sq[:, 2 * t + 1:2 * t + 2], scalar=1.0 / D,
                                                   in1=mean_of_t, op0=ALU.mult, op1=ALU.add).then_inc(x3_ms, 1)

            x3(0, 0)
            x3(0, 1)
            dve.wait_ge(gf_loaded, 16)
            gained(0)
            mean(0, 0)
            mean(0, 1)
            x3(1, 0)
            y(0)
            x3(1, 1)
            gained(1)
            mean(1, 0)
            mean(1, 1)
            y(1)

        @block.tensor
        def _(pe):
            def transposed(view_hi, view_lo, moving, col, into, ready=None, tiles=None):
                k_tiles = view_hi.shape[1]
                for k in tiles or range(k_tiles):
                    if ready:
                        made, before, per = ready
                        if k % per == 0:
                            pe.wait_ge(made, before + k // per + 1)
                    whole = (into[:, :], view_hi[:, k, col:col + P], moving[:, k, :, :])
                    left = (into[:, 0:T], view_lo[:, k, col:col + P], moving[:, k, 0, :])
                    if k < k_tiles - 1:
                        nc.tensor.matmul(*whole, start=(k == 0), stop=False)
                        ins = nc.tensor.matmul(*left, start=False, stop=False)
                    else:
                        nc.tensor.matmul(*left, start=False, stop=False)
                        ins = nc.tensor.matmul(*whole, start=False, stop=True)
                return ins

            def unit_ready(slot, rnd):
                pe.wait_ge(lo_made, SLOTS * rnd + slot + 1)

            def output_free(o):
                if o >= 2:
                    pe.wait_ge(out_read, o - 1)

            def half_wide(slot, moving, parity, n, ready=None, tiles=None):
                return transposed(wide(w_hi, slot), wide(w_lo, slot), moving, n * P, pair[parity][:, n, :],
                                  ready, tiles)

            def wide_unit(slot, rnd, moving, parity, ready=None):
                unit_ready(slot, rnd)
                half_wide(slot, moving, parity, 0, ready)
                half_wide(slot, moving, parity, 1).then_inc(units_used, 1)

            def natural_unit(u, moving, parity, half, between=None):
                slot = u % SLOTS
                unit_ready(*unit(u))
                hi, lo = mid(w_hi, slot), mid(w_lo, slot)
                for t in range(2):
                    for k in range(4):
                        for n, (part, w) in enumerate(((0, hi), (0, lo), (1, hi))):
                            ins = nc.tensor.matmul(pair[parity][:, t, :],
                                                   moving[:, 4 * half + k, part, t * P:(t + 1) * P], w[:, k, :],
                                                   start=(half == 0 and k == 0 and n == 0),
                                                   stop=(half == 1 and k == 3 and n == 2))
                    if t == 0 and between:
                        between()
                ins.then_inc(units_used, 1)

            pe.wait_ge(ones_made, 1)
            for i in range(WARM_UP):
                nc.tensor.matmul(p_logits[:, 0:P], ones[:, :], ones[:, :], start=True, stop=True)
            pe.wait_ge(ident_loaded, 16)

            def x_turn(n):
                pe.wait_ge(x_loaded[n], 16)
                for k in range(4 * n, 4 * n + 4):
                    for t in range(2):
                        ins = nc.tensor.transpose(x_first(k)[:, t * P:(t + 1) * P],
                                                  nat_b[:, t, k * P:(k + 1) * P], ident[:, :])
                    ins.then_inc(xt_made, 1)

            x_turn(0)
            pe.wait_ge(g1_loaded, 16)
            nc.tensor.transpose(pair[0][:, 1, 0:8], g1_rows[:, :], ident[0:8, 0:8]).then_inc(cols_t, 1)
            for i in range(WARM_GAP):
                nc.tensor.matmul(pair[0][:, 0, 0:P], ones[:, :], ones[:, :], start=True, stop=True)

            def factors_row():
                pe.wait_ge(diag_made, 2)
                pe.wait_ge(xt_lo, KD)
                nc.tensor.matmul(p_logits[:, 0:T], ones[:, :], diag, start=True, stop=True).then_inc(row_t, 1)

            for u in range(FIRST_UNITS):
                output_free(O_QK + u)
                for k in range(KD):
                    if k % 2 == 0:
                        pe.wait_ge(lo_made if k == 6 else first_lo, part_count(u, k // 2))
                    for n in range(2):
                        ins = half_wide(u, act_a, u % 2, n, (xt_lo, 0, 1) if u == 0 else None, [k])
                    if u == 0 and k == 0:
                        x_turn(1)
                ins.then_inc(units_used, 1)
                if u == 1:
                    factors_row()
            for u in range(FIRST_UNITS, U_NAT):
                o = O_QK + u
                output_free(o)
                wide_unit(*unit(u), act_a, o % 2)

            def first_scores():
                pe.wait_ge(scaled_made, O_QK + 8)
                pe.wait_ge(row_made, 1)
                pe.wait_ge(xt_lo, KD)
                pe.wait_ge(rows_loaded, 32)
                nc.tensor.transpose(p_retv[:, 0:24], rows[:, :], ident[0:24, 0:24]).then_inc(cols_t, 1)
                moba_scores(0)
                ret_scores_of(0)

            def moba_scores(h):
                if h:
                    pe.wait_ge(logits_read, h)
                a, q, k = (h % 2) * MOBA_DIM, 8 + h // 2, 12 + h // 2
                nc.tensor.matmul(p_logits[:, 0:P], qk[a:a + MOBA_DIM, q, 0:P], qk[a:a + MOBA_DIM, k, 0:P],
                                 start=True, stop=True)
                nc.tensor.matmul(p_logits[:, P:3 * P], qk[a:a + MOBA_DIM, q, P:T], qk[a:a + MOBA_DIM, k, :],
                                 start=True, stop=True).then_inc(logits_made, 1)

            def moba_transposes(h):
                pe.wait_ge(probs_normed, 2 * h + 2)
                if h:
                    pe.wait_ge(moba_read, h)
                for b in range(3):
                    ins = nc.tensor.transpose(p_moba[:, b * P:(b + 1) * P], scratch[:, b * P:(b + 1) * P], ident[:, :])
                ins.then_inc(pt_made, 1)

            def moba_values(h):
                pe.wait_ge(pt_read, h + 1)
                a = (h % 2) * MOBA_DIM
                v = nat_c[:, :, h * MOBA_DIM:(h + 1) * MOBA_DIM]
                nc.tensor.matmul(p_moba[a:a + MOBA_DIM, 0:T], v[:, 0, :], probs_t[:, 0:T], start=True, stop=False)
                nc.tensor.matmul(p_moba[a:a + MOBA_DIM, P:T], v[:, 1, :], probs_t[:, T:T + P], start=False, stop=True
                                 ).then_inc(moba_made, 1)

            def ret_scores_of(j):
                if j >= 1:
                    pe.wait_ge(rs_read, 2 * j)
                nc.tensor.matmul(p_ret[:, 0:T], qk[:, 4 + j, 0:P], qk[:, j, :], start=True, stop=True)
                nc.tensor.matmul(p_ret[:, T:T + P], qk[:, 4 + j, P:T], qk[:, j, P:T], start=True, stop=True
                                 ).then_inc(rs_made, 1)

            def ret_values(j):
                pe.wait_ge(rs_read, 2 * j + 2)
                if j:
                    pe.wait_ge(rt_lo, j)
                else:
                    pe.wait_ge(cols_made, 2)
                v = nat_b[:, :, j * RET_V:(j + 1) * RET_V]
                nc.tensor.matmul(p_retv[:, 0:RET_V], ret_scores[:, 0:P], v[:, 0, :], start=True, stop=True)
                nc.tensor.matmul(p_retv[:, RET_V:], ret_scores[:, P:T], v[:, 0, :], start=True, stop=False)
                nc.tensor.matmul(p_retv[:, RET_V:], ret_scores[:, T:T + P], v[:, 1, :], start=False, stop=True
                                 ).then_inc(rv_made, 1)

            def ret_turn(j):
                pe.wait_ge(ret_done, j + 1)
                for k in range(2):
                    for t in range(2):
                        a = j * RET_V + k * P
                        ins = nc.tensor.transpose(p_retv[:, k * T + t * P:k * T + (t + 1) * P],
                                                  nat_a[:, t, a:a + P], ident[:, :])
                ins.then_inc(rt_made, 1)

            for u in range(U_NAT, U_GATE):
                n, half = divmod(u - U_NAT, 2)
                o = O_NAT + n
                if half == 0:
                    output_free(o)
                natural_unit(u, act_a, o % 2, half)
                if u == U_GATE - 2:
                    first_scores()

            for i in range(MOBA_HEADS):
                slot, rnd = unit(U_GATE + i)
                o = O_GATE + i
                output_free(o)
                unit_ready(slot, rnd)
                half_wide(slot, act_a, o % 2, 0)
                moba_transposes(i)
                if i == 0:
                    pe.wait_ge(out_read, O_GATE)
                if i % 2 == 0:
                    ret_values(i // 2)
                else:
                    ret_turn(i // 2)
                if i + 1 < MOBA_HEADS:
                    moba_scores(i + 1)
                half_wide(slot, act_a, o % 2, 1).then_inc(units_used, 1)
                if i % 2 == 1 and i + 1 < MOBA_HEADS:
                    ret_scores_of(i // 2 + 1)
                moba_values(i)

            for u in range(U_RET, U_MOBA):
                o = O_RET + u - U_RET
                output_free(o)
                wide_unit(*unit(u), act_b, o % 2, (rt_lo, 0, 2) if u == U_RET else None)

            for u in range(U_MOBA, U_OUT):
                slot = u % SLOTS
                unit_ready(*unit(u))
                for n in range(4):
                    o = O_MOBA + 2 * (u - U_MOBA) + n // 2
                    if n % 2 == 0:
                        output_free(o)
                    if u == U_MOBA and n == 0:
                        pe.wait_ge(mt_lo, 4)
                    ins = transposed(mid(w_hi, slot), mid(w_lo, slot), act_c, n * P, pair[o % 2][:, n % 2, :])
                    if n == 1:
                        ins.then_inc(half_made, 1)
                ins.then_inc(units_used, 1)

            def x2_turn(n):
                if n:
                    pe.wait_ge(xt_lo, KD + 4)
                for t in range(2):
                    pe.wait_ge(x2_made, 2 * n + t + 1)
                    for k in range(4 * n, 4 * n + 4):
                        ins = nc.tensor.transpose(x_bank(k)[:, t * P:(t + 1) * P],
                                                  nat_b[:, t, k * P:(k + 1) * P], ident[:, :])
                        if t == 1:
                            ins.then_inc(xt_made, 1)

            for u in range(U_OUT, U_MLP):
                half, n = divmod(u - U_OUT, 2)
                if half == 0:
                    output_free(O_OUT + n)
                pe.wait_ge(merged_lo, 2 * half + 2)
                natural_unit(u, act_a, (O_OUT + n) % 2, half,
                             between=(lambda: x2_turn(0)) if u == U_MLP - 1 else None)

            def up_unit(kind, c, half):
                wide_unit(kind[0], kind[1] + c, act_b, (O_UP + half) % 2)

            def down_unit(at, c, half, first=False, final=False):
                slot = at[0]
                unit_ready(*at)
                pe.wait_ge(hid_lo, 2 * c + 1 + half)
                hi, lo = long(w_hi, slot), long(w_lo, slot)

                def product(t, f, part, w, n, start=False, stop=False):
                    return nc.tensor.matmul(bank[2 * t + n][:, :], act_c[:, 2 * half + f, part, t * P:(t + 1) * P],
                                            w[:, f, n * 512:(n + 1) * 512], start=start, stop=stop)

                for t in range(2):
                    if final:
                        for n in range(2):
                            for f in range(2):
                                product(t, f, 0, hi, n)
                                product(t, f, 0, lo, n)
                                ins = product(t, f, 1, hi, n, stop=(f == 1))
                            ins.then_inc(down_made, 1)
                        continue
                    for f in range(2):
                        for n in range(2):
                            product(t, f, 0, hi, n, start=(first and f == 0))
                            product(t, f, 0, lo, n)
                        for n in range(2):
                            ins = product(t, f, 1, hi, n)
                if not final:
                    ins.then_inc(units_used, 1)

            for part in range(2):
                for half in range(2):
                    slot, rnd = unit(U_MLP + half)
                    if part == 0:
                        unit_ready(slot, rnd)
                        pe.wait_ge(x2_made, 2 + 2 * half)
                    for n in range(2):
                        ins = half_wide(slot, act_b, (O_UP + half) % 2, n, (xt_lo, KD, 1),
                                        range(4 * part, 4 * part + 4))
                    if part == 0 and half == 0:
                        x2_turn(1)
                    if part == 1:
                        ins.then_inc(units_used, 1)

            def mlp_round(c, first):
                pe.wait_ge(out_read, O_OUT + 2 * c + 1)
                up_unit(UP_A, c, 0)
                down_unit((DOWN_A[0], DOWN_A[1] + c), c, 0, first=first)
                pe.wait_ge(out_read, O_OUT + 2 * c + 2)
                up_unit(UP_B, c, 1)
                down_unit((DOWN_B[0], DOWN_B[1] + c), c, 1)

            mlp_round(0, True)
            with pe.Fori(1, MLP_CHUNKS - 1) as c:
                mlp_round(c, False)
            down_unit(LAST_A, MLP_CHUNKS - 1, 0)
            down_unit(LAST_B, MLP_CHUNKS - 1, 1, final=True)


def kernel(x, norm1_g, w_in, b_gate, w_ret_o, w_moba_o, w_out, norm2_g, w_up, w_down, normf_g):
    import numpy as np

    import concourse.bacc as bacc
    from concourse.bass_utils import run_bass_kernel_spmd

    given = {
        "x": x, "norm1_g": norm1_g, "w_in": w_in, "b_gate": b_gate, "w_ret_o": w_ret_o, "w_moba_o": w_moba_o,
        "w_out": w_out, "norm2_g": norm2_g, "w_up": w_up, "w_down": w_down, "normf_g": normf_g,
        "consts": constants(),
    }
    nc = bacc.Bacc("TRN2", target_bir_lowering=False, num_devices=1)
    arrays, args = {}, []
    for name, value in given.items():
        a = np.ascontiguousarray(value)
        arrays[f"{name}_dram"] = a
        args.append(nc.dram_tensor(f"{name}_dram", a.shape, mybir.dt.from_np(a.dtype), kind="ExternalInput").ap())
    args.append(nc.dram_tensor("out_dram", (1, T, D), F32, kind="ExternalOutput").ap())
    hybrid_block(nc, *args)
    r = run_bass_kernel_spmd(nc, [arrays], core_ids=[0])
    return r.results[0]["out_dram"]
```
